# Optimizing a Trainium2 kernel written in Bass

```python
import jax, jax.numpy as jnp
from jax import lax
import numpy as np

D_MODEL = 1024
BATCH = 1
SEQ = 512
DEPTH = 1
DEC_BATCH = 1
DEC_SEQ = 256
PAST_LEN = 128

HEAD_DIM = 64
A_Q_HEADS = 8
A_KV_HEADS = 2
A_GROUP = A_Q_HEADS // A_KV_HEADS
B_WINDOWS = (128, 512, 2048)
B_DILATIONS = (1, 4, 16)
B_N_GROUPS = len(B_WINDOWS)
B_HEADS_PER_GROUP = 4
B_HEADS = B_N_GROUPS * B_HEADS_PER_GROUP
D_FF = 4 * D_MODEL
GRID_W = 64
AXIAL_THETA = 10000.0
PARTIAL_THETA = 500000.0
PARTIAL_ROPE_DIM = HEAD_DIM // 4
Q_BLOCK = 128
EPS = 1e-6

A_Q_W = A_Q_HEADS * HEAD_DIM
A_KV_W = A_KV_HEADS * HEAD_DIM
B_W = B_HEADS * HEAD_DIM
B_OUT_W = B_HEADS_PER_GROUP * HEAD_DIM
IN_SPLITS = (A_Q_W, A_KV_W, A_KV_W, B_W, B_W, B_W, D_MODEL, D_MODEL)
IN_W = sum(IN_SPLITS)

kernel_name = "hybrid_axial_gqa_dilated_encoder"

def rmsnorm(x, g):
    xf = x.astype(jnp.float32)
    y = xf * lax.rsqrt(jnp.mean(xf * xf, axis=-1, keepdims=True) + EPS)
    return (y * g.astype(jnp.float32)).astype(x.dtype)

def rope(x, pos, theta):
    d = x.shape[-1]
    d2 = d // 2
    freqs = theta ** (-(jnp.arange(d2, dtype=jnp.float32) * 2.0) / d)
    ang = pos.astype(jnp.float32)[:, None] * freqs[None, :]
    bshape = (pos.shape[0],) + (1,) * (x.ndim - 3) + (d2,)
    cos = jnp.cos(ang).reshape(bshape)
    sin = jnp.sin(ang).reshape(bshape)
    xf = x.astype(jnp.float32)
    x1, x2 = xf[..., :d2], xf[..., d2:]
    return jnp.concatenate([x1 * cos - x2 * sin, x2 * cos + x1 * sin], axis=-1).astype(x.dtype)

def axial_gqa(q, k, v, q_gain, k_gain):
    Bn, S = q.shape[0], q.shape[1]
    rows = S // GRID_W
    r, c = jnp.meshgrid(jnp.arange(rows), jnp.arange(GRID_W), indexing="ij")
    r = r.reshape(-1)
    c = c.reshape(-1)
    q = rmsnorm(q, q_gain)
    k = rmsnorm(k, k_gain)
    half = HEAD_DIM // 2

    def axial(t):
        return jnp.concatenate([rope(t[..., :half], r, AXIAL_THETA),
                                rope(t[..., half:], c, AXIAL_THETA)], axis=-1)

    q = axial(q)
    k = axial(k)
    nb = S // Q_BLOCK
    qb = q.reshape(Bn, nb, Q_BLOCK, A_KV_HEADS, A_GROUP, HEAD_DIM).transpose(1, 0, 2, 3, 4, 5)
    scale = HEAD_DIM ** -0.5

    def block(qi):
        s = jnp.einsum("bqkgd,bskd->bkgqs", qi, k).astype(jnp.float32) * scale
        p = jax.nn.softmax(s, axis=-1)
        return jnp.einsum("bkgqs,bskd->bqkgd", p.astype(v.dtype), v)

    o = lax.map(block, qb)
    return o.transpose(1, 0, 2, 3, 4, 5).reshape(Bn, S, A_Q_W)

def dilated_attention(q, k, v):
    Bn, S = q.shape[0], q.shape[1]
    t = jnp.arange(S)

    def prope(x):
        return jnp.concatenate([rope(x[..., :PARTIAL_ROPE_DIM], t, PARTIAL_THETA),
                                x[..., PARTIAL_ROPE_DIM:]], axis=-1)

    q = prope(q)
    k = prope(k)
    offs = jnp.stack([jnp.arange(-(w // 2) // d, (w // 2) // d + 1) * d
                      for w, d in zip(B_WINDOWS, B_DILATIONS)])
    nb = S // Q_BLOCK
    qb = q.reshape(Bn, nb, Q_BLOCK, B_N_GROUPS, B_HEADS_PER_GROUP, HEAD_DIM).transpose(1, 0, 2, 3, 4, 5)
    starts = jnp.arange(nb) * Q_BLOCK
    g_idx = jnp.arange(B_N_GROUPS)[None, :, None]
    scale = HEAD_DIM ** -0.5

    def block(args):
        qi, s0 = args
        idx = s0 + jnp.arange(Q_BLOCK)[:, None, None] + offs[None]
        valid = (idx >= 0) & (idx < S)
        idxc = jnp.clip(idx, 0, S - 1)
        kg = k[:, idxc, g_idx]
        vg = v[:, idxc, g_idx]
        s = jnp.einsum("bqghd,bqgjhd->bqghj", qi, kg).astype(jnp.float32) * scale
        s = jnp.where(valid[None, :, :, None, :], s, -jnp.inf)
        m = jnp.max(s, axis=-1, keepdims=True)
        p = jnp.exp(s - m)
        den = jnp.sum(p, axis=-1, keepdims=True)
        o = jnp.einsum("bqghj,bqgjhd->bqghd", (p / den).astype(v.dtype), vg)
        lse = (m + jnp.log(den))[..., 0]
        w = jax.nn.softmax(lse, axis=2)
        return jnp.einsum("bqgh,bqghd->bqhd", w.astype(o.dtype), o)

    o = lax.map(block, (qb, starts))
    return o.transpose(1, 0, 2, 3, 4).reshape(Bn, S, B_OUT_W)

def layer(x, w_in, w_a_out, w_b_out, w_out, g_mix, q_gain, k_gain, g_mlp, w_up, w_down):
    Bn, S, _ = x.shape
    h = rmsnorm(x, g_mix)
    z = h @ w_in
    cuts = [int(c) for c in np.cumsum(IN_SPLITS)[:-1]]
    qa, ka, va, qb, kb, vb, ga, gb = jnp.split(z, cuts, axis=-1)
    ya = axial_gqa(qa.reshape(Bn, S, A_Q_HEADS, HEAD_DIM),
                   ka.reshape(Bn, S, A_KV_HEADS, HEAD_DIM),
                   va.reshape(Bn, S, A_KV_HEADS, HEAD_DIM), q_gain, k_gain) @ w_a_out
    bshape = (Bn, S, B_N_GROUPS, B_HEADS_PER_GROUP, HEAD_DIM)
    yb = dilated_attention(qb.reshape(bshape), kb.reshape(bshape), vb.reshape(bshape)) @ w_b_out
    mixed = jax.nn.sigmoid(ga) * ya + jax.nn.sigmoid(gb) * yb
    x = x + mixed @ w_out
    h = rmsnorm(x, g_mlp)
    u = jnp.square(jax.nn.relu(h @ w_up))
    return x + u @ w_down

def trunk(x, w_in, w_a_out, w_b_out, w_out, g_mix, q_gain, k_gain, g_mlp, w_up, w_down, g_final):
    for l in range(DEPTH):
        x = layer(x, w_in[l], w_a_out[l], w_b_out[l], w_out[l], g_mix[l], q_gain[l], k_gain[l],
                  g_mlp[l], w_up[l], w_down[l])
    return rmsnorm(x, g_final)

def setup_inputs(seed: int = 0) -> dict:
    key = jax.random.key(seed)
    ks = jax.random.split(key, 13)
    f32 = jnp.float32

    def w(k, shape, fan_in):
        return jax.random.normal(k, shape, f32) * (fan_in ** -0.5)

    def gain(k, shape):
        return 1.0 + 0.02 * jax.random.normal(k, shape, f32)

    return {
        "x_prompt": jax.random.normal(ks[0], (BATCH, SEQ, D_MODEL), f32),
        "x_sample": jax.random.normal(ks[1], (DEC_BATCH, DEC_SEQ, D_MODEL), f32),
        "w_in": w(ks[2], (DEPTH, D_MODEL, IN_W), D_MODEL),
        "w_a_out": w(ks[3], (DEPTH, A_Q_W, D_MODEL), A_Q_W),
        "w_b_out": w(ks[4], (DEPTH, B_OUT_W, D_MODEL), B_OUT_W),
        "w_out": w(ks[5], (DEPTH, D_MODEL, D_MODEL), D_MODEL),
        "g_mix": gain(ks[6], (DEPTH, D_MODEL)),
        "q_gain": gain(ks[7], (DEPTH, HEAD_DIM)),
        "k_gain": gain(ks[8], (DEPTH, HEAD_DIM)),
        "g_mlp": gain(ks[9], (DEPTH, D_MODEL)),
        "w_up": w(ks[10], (DEPTH, D_MODEL, D_FF), D_MODEL),
        "w_down": w(ks[11], (DEPTH, D_FF, D_MODEL), D_FF),
        "g_final": gain(ks[12], (D_MODEL,)),
    }

def reference(x_prompt, x_sample, w_in, w_a_out, w_b_out, w_out, g_mix, q_gain, k_gain,
              g_mlp, w_up, w_down, g_final):
    y_prompt = trunk(x_prompt, w_in, w_a_out, w_b_out, w_out, g_mix, q_gain, k_gain,
                     g_mlp, w_up, w_down, g_final)
    y_sample = trunk(x_sample, w_in, w_a_out, w_b_out, w_out, g_mix, q_gain, k_gain,
                     g_mlp, w_up, w_down, g_final)
    return (y_prompt, y_sample)


_drawn_inputs = setup_inputs


def setup_inputs(seed=0):
    import zlib

    import numpy as np

    out = dict(_drawn_inputs(seed))
    spreads = {}
    factors = {'g_mix': 8.0, 'q_gain': 8.0, 'k_gain': 8.0, 'g_mlp': 9.121, 'g_final': 8.251}
    for name, (base, spread) in spreads.items():
        noise = np.random.default_rng([zlib.crc32(name.encode()), seed]).standard_normal(out[name].shape)
        drawn = base * np.exp(spread * noise) if base else spread * noise
        out[name] = __import__('jax').numpy.asarray(drawn.astype(out[name].dtype))
    for name, factor in factors.items():
        out[name] = (out[name] * factor).astype(out[name].dtype)
    return out
```

```python
from contextlib import ExitStack

import numpy as np

import concourse.bass as bass
from concourse import mybir

F32 = mybir.dt.float32
F32R = mybir.dt.float32r
ALU = mybir.AluOpType
ACT = mybir.ActivationFunctionType
AX_X = mybir.AxisListType.X

P = 128
D = 1024
KC = D // P
TILES, PROMPT_TILES = 6, 4
TOK = TILES * P
PROMPT, SAMPLE = 512, 256
HALF = TOK // 2
HD = 64
A_HEADS, A_KV, A_GROUP = 8, 2, 4
B_HEADS, B_GROUPS = 4, 3
FF = 4096
COLS = 512
EPS = 1e-6
SCALE = HD ** -0.5
RING, RAW = 16, 4
MLP_STEPS = FF // COLS
NEG = -1.0e30

Q_A, K_A, V_A, Q_B, K_B, V_B, G_A, G_B = 0, 512, 640, 768, 1536, 2304, 3072, 4096
GW = B_HEADS * HD

STAT_A = TILES * A_HEADS
STAT_B = TILES * B_HEADS
STATS = STAT_A + B_GROUPS * STAT_B


def weight_blocks():
    def full(name, matrix, col, rows):
        return (name, [[(matrix, k * P, col, COLS)] for k in range(rows // P)])

    def paired(name, cols):
        return (name, [[("w_in", k * P, c, COLS // len(cols)) for c in cols] for k in range(KC)])

    blocks = [full("qa", "w_in", Q_A, D), paired("kva", [K_A, V_B]), paired("qk0", [Q_B, K_B]),
              full("v12", "w_in", V_B + GW, D), paired("qk1", [Q_B + GW, K_B + GW]),
              paired("qk2", [Q_B + 2 * GW, K_B + 2 * GW])]
    gate_a = [full(f"ga{j}", "w_in", G_A + j * COLS, D) for j in range(2)]
    gate_b = [full(f"gb{j}", "w_in", G_B + j * COLS, D) for j in range(2)]
    out_a = [full(f"ya{j}", "w_a_out", j * COLS, A_HEADS * HD) for j in range(2)]
    out_b = [full(f"yb{j}", "w_b_out", j * COLS, B_HEADS * HD) for j in range(2)]
    blocks += [gate_a[0], out_a[0], gate_b[0], out_b[0], gate_b[1], out_b[1], gate_a[1], out_a[1]]
    blocks += [full(f"wo{j}", "w_out", j * COLS, D) for j in range(2)]
    return blocks


def attention_units():
    branch_a, band, classes = [], [], []
    for t in range(PROMPT_TILES):
        branch_a += [("A", t, [(h, 0, 4)]) for h in range(A_HEADS)]
    for t in range(PROMPT_TILES, TILES):
        branch_a += [("A", t, [(h, 4, 2), (h + 1, 4, 2)]) for h in range(0, A_HEADS, 2)]
    for t in range(PROMPT_TILES):
        lo, hi = max(0, t - 1), min(PROMPT_TILES - 1, t + 1)
        band += [("0", t, [(h, lo, hi - lo + 1)]) for h in range(B_HEADS)]
    for t in range(PROMPT_TILES, TILES):
        band += [("0", t, [(h, 4, 2), (h + 1, 4, 2)]) for h in range(0, B_HEADS, 2)]
    for g in "12":
        classes += [(g, t, [(h, t, 1) for h in range(B_HEADS)]) for t in range(TILES)]
    return branch_a, band, classes


def make_schedule():
    blocks = weight_blocks()
    sizes = {name: len(chunks) for name, chunks in blocks}
    owner = [name for name, chunks in blocks for _ in chunks]
    branch_a, band, classes = attention_units()
    steps, units, finished, turned = [], [], set(), set()
    state = {"cut": 0, "tick": 0}

    def cuts(limit):
        for _ in range(limit):
            n = state["cut"]
            if n < len(owner) and (n < RING or owner[n - RING] in finished):
                steps.append(("hi", n))
                state["cut"] += 1

    def unit(name, i, count):
        need = len(owner) - owner[::-1].index(name)
        cuts(max(0, need - state["cut"]))
        assert state["cut"] >= need
        steps.append(("unit", name, i))
        if i == count - 1:
            finished.add(name)
        cuts(2)

    def next_unit():
        if branch_a:
            last_keys = branch_a[0][2][0][1] + branch_a[0][2][0][2] - 1
            return branch_a.pop(0) if ("kva", last_keys) in turned else None
        if classes and ("qk" + classes[0][0], classes[0][1]) in turned:
            return classes.pop(0)
        if band and ("qk0", TILES - 1) in turned:
            return band.pop(0)
        return None

    def attend(count):
        for _ in range(count):
            if branch_a or band or classes:
                new = next_unit()
                if new is None:
                    return
                units.append(new)
            i = state["tick"]
            if 0 <= i - 2 < len(units):
                steps.append(("turn_p", i - 2))
            if i < len(units):
                steps.append(("scores", i))
            if 0 <= i - 3 < len(units):
                steps.append(("pv", i - 3))
            state["tick"] += 1

    waiting = []

    def turn_next():
        b, t = waiting.pop(0)
        steps.append(("turn_qk", b, t))
        turned.add((b, t))

    def rotated_unit(name, t):
        unit(name, t, TILES)
        waiting.append((name, t))
        while len(waiting) > 2:
            turn_next()

    steps.append(("norm", 0))
    cuts(2)
    steps.append(("norm", 1))
    for t in range(TILES):
        cuts(3)
        steps += [("turn", t, 0), ("turn", t, 1)]
        if t + 2 < TILES:
            steps.append(("norm", t + 2))
        if t >= 1:
            rotated_unit("qa", t - 1)
    rotated_unit("qa", TILES - 1)
    for name, rate in (("kva", 3), ("qk0", 3), ("v12", 3), ("qk1", 3), ("qk2", 3)):
        for t in range(TILES):
            if name == "v12":
                unit(name, t, TILES)
                if waiting:
                    turn_next()
            else:
                rotated_unit(name, t)
            attend(rate)
    while waiting:
        turn_next()
        attend(1)
    while band:
        attend(1)
    for i in range(8):
        unit("ga0", i, 8)
        attend(1)
    while state["tick"] < len(units) + 3:
        attend(1)
    steps.append(("send_stats",))
    steps += [("turn_a", t) for t in range(TILES)]
    for i in range(8):
        unit("ya0", i, 8)
    for i in range(8):
        unit("gb0", i, 8)
        if i == 1:
            steps.append(("combine",))
    steps += [("turn_b", s, c) for s in range(2) for c in range(2)]
    for name in ("yb0", "gb1", "yb1", "ga1"):
        for i in range(8):
            unit(name, i, 8)
    after = {0: [0], 1: [1, 4], 2: [2], 3: [3, 5], 5: [6], 7: [7]}
    for i in range(8):
        unit("ya1", i, 8)
        steps += [("split_mix", c) for c in after.get(i, [])]
    steps.append(("load_x",))
    for i in range(TILES):
        unit("wo0", i, TILES)
    for i in range(TILES):
        unit("wo1", i, TILES)
        steps.append(("norm2", i))
        if i < 4:
            steps += [("hi_up", 2 * i), ("hi_up", 2 * i + 1)]
        if i >= 2:
            steps += [("turn2", i - 2, 0), ("turn2", i - 2, 1)]
    steps += [("turn2", t, half) for t in (TILES - 2, TILES - 1) for half in range(2)]
    assert state["cut"] == len(owner) and not (branch_a or band or classes)
    return blocks, units, steps


class Plan:

    def __init__(self):
        self.blocks, self.units, self.steps = make_schedule()
        self.chunks = [c for _, chunks in self.blocks for c in chunks]
        self.start, self.index, self.size = {}, {}, {}
        n = 0
        for b, (name, chunks) in enumerate(self.blocks):
            self.start[name], self.index[name], self.size[name] = n, b, len(chunks)
            n += len(chunks)
        self.owner = [b for b, (_, chunks) in enumerate(self.blocks) for _ in chunks]
        self.unit_no, self.turn_no, self.qk_no = {}, {}, {}
        self.split_no = {}
        for s in self.steps:
            if s[0] == "unit":
                self.unit_no[s] = len(self.unit_no)
            elif s[0] in ("turn", "turn_qk", "turn_p", "turn_a", "turn_b", "turn2"):
                self.turn_no[s] = len(self.turn_no)
                if s[0] == "turn_qk":
                    self.qk_no[s] = len(self.qk_no)
                elif s[0] != "turn_p":
                    self.split_no[s] = len(self.split_no)
        self.raw_count, filled = [], [0] * RAW
        for n, c in enumerate(self.chunks):
            filled[n % RAW] += 16 * len(c)
            self.raw_count.append(filled[n % RAW])
        self.raw_total = filled


def stat_col(branch, t, h):
    return t * A_HEADS + h if branch == "A" else STAT_A + int(branch) * STAT_B + t * B_HEADS + h


def build(nc, x_prompt, x_sample, w_in, w_a_out, w_b_out, w_out, g_mix, q_gain, k_gain, g_mlp, w_up,
          w_down, g_final, rope_a_tab, rope_b_tab, mask_tab, ident_tab, y_prompt, y_sample):
    plan = Plan()
    blocks, units, steps = plan.blocks, plan.units, plan.steps
    matrices = {"w_in": w_in[0], "w_a_out": w_a_out[0], "w_b_out": w_b_out[0], "w_out": w_out[0]}
    w_up, w_down = w_up[0], w_down[0]

    def x_rows(t):
        return x_prompt[0, t * P:(t + 1) * P, :] if t < PROMPT_TILES \
            else x_sample[0, (t - PROMPT_TILES) * P:(t - PROMPT_TILES + 1) * P, :]

    def y_rows(t):
        return y_prompt[0, t * P:(t + 1) * P, :] if t < PROMPT_TILES \
            else y_sample[0, (t - PROMPT_TILES) * P:(t - PROMPT_TILES + 1) * P, :]

    with ExitStack() as ctx:
        def sb(stack, name, shape, dt=F32):
            return stack.enter_context(nc.sbuf_tensor(name, shape, dt))

        def sem(name):
            return ctx.enter_context(nc.semaphore(name))

        ring_hi = sb(ctx, "ring_hi", [P, RING, COLS], F32R)
        ring_lo = sb(ctx, "ring_lo", [P, RING, COLS], F32R)
        raw = sb(ctx, "raw", [P, RAW, COLS])
        act_hi = sb(ctx, "act_hi", [P, KC, TOK], F32R)
        act_lo = sb(ctx, "act_lo", [P, KC, TOK], F32R)
        ident = sb(ctx, "ident", [P, P])
        band_mask = sb(ctx, "band_mask", [P, 3 * P])
        class_mask = sb(ctx, "class_mask", [P, 3, 8])
        rope_qc = sb(ctx, "rope_qc", [P, PROMPT_TILES, HD])
        rope_qs = sb(ctx, "rope_qs", [P, PROMPT_TILES, HD])
        rope_kc = sb(ctx, "rope_kc", [P, PROMPT_TILES, HD])
        rope_ks = sb(ctx, "rope_ks", [P, PROMPT_TILES, HD])
        rope_b = sb(ctx, "rope_b", [P, 10, 2, 16])
        neg_max = sb(ctx, "neg_max", [P, STATS])
        den = sb(ctx, "den", [P, STATS])
        eps = sb(ctx, "eps", [P, 1])
        ssq = sb(ctx, "ssq", [P, 2])
        rms = sb(ctx, "rms", [P, 2])
        qk_ssq = sb(ctx, "qk_ssq", [P, 8])
        qk_rms = sb(ctx, "qk_rms", [P, 8])

        st = ExitStack()
        x_in = sb(st, "x_in", [P, TILES, D])
        gain_bc = sb(st, "gain_bc", [P, D])
        xn = sb(st, "xn", [P, 2, D])
        st.close()

        st = ExitStack()
        qT_a = sb(st, "qT_a", [P, 4, TOK])
        kT_a = sb(st, "kT_a", [P, TOK])
        v_a = sb(st, "v_a", [P, TILES, A_KV * HD])
        o_a = sb(st, "o_a", [P, TILES, A_HEADS * HD])
        probs = sb(st, "probs", [P, 2, 512])
        probsT = sb(st, "probsT", [P, 2, 512])
        tok = sb(st, "tok", [P, 2, 512])
        rot = sb(st, "rot", [P, 512])
        qkT_c = sb(st, "qkT_c", [P, 2, 512])
        v_b = sb(st, "v_b", [P, TILES, B_GROUPS * GW])
        qkT_0 = sb(st, "qkT_0", [P, 4, TOK])
        st.close()
        st = ExitStack()
        sb(st, "hold_r", [P, 49152 // 4])
        rope_raw = sb(st, "rope_raw", [P, 2, PROMPT_TILES, HD])
        qk_gain = sb(st, "qk_gain", [P, 2, HD])
        st.close()

        st = ExitStack()
        o_b = sb(st, "o_b", [P, B_GROUPS, TILES, GW])
        st.close()
        st = ExitStack()
        sb(st, "hold_o", [P, (18432 + 12288) // 4])
        oTa_hi = sb(st, "oTa_hi", [P, 4, TOK], F32R)
        oTa_lo = sb(st, "oTa_lo", [P, 4, TOK], F32R)
        oTb_hi = sb(st, "oTb_hi", [P, 2, TOK], F32R)
        oTb_lo = sb(st, "oTb_lo", [P, 2, TOK], F32R)
        gate = sb(st, "gate", [P, 4, TOK])
        st.close()
        st = ExitStack()
        mixed_1 = sb(st, "mixed_1", [P, 4, TOK])
        mix_part = sb(st, "mix_part", [P, 2, HALF])
        sb(st, "hold_m", [P, 3072 // 4])
        mixed_0 = sb(st, "mixed_0", [P, 4, TOK])
        st.close()
        mixed = (mixed_0, mixed_1)

        st = ExitStack()
        u_hi = sb(st, "u_hi", [P, 4, TOK], F32R)
        u_lo = sb(st, "u_lo", [P, 4, TOK], F32R)
        relu = sb(st, "relu", [P, 2, HALF])
        usq = sb(st, "usq", [P, 2, HALF])
        x2 = sb(st, "x2", [P, TILES, D])
        gain_mlp = sb(st, "gain_mlp", [P, D])
        gain_fin = sb(st, "gain_fin", [P, D])
        xn2 = sb(st, "xn2", [P, 2, D])
        st.close()

        stats_c = rope_qc[:].rearrange("p t d -> p (t d)")[:, 0:96].rearrange("p (t c) -> p t c", c=16)
        stats_n = rope_qc[:].rearrange("p t d -> p (t d)")[:, 96:192].rearrange("p (t c) -> p t c", c=16)
        w_0 = rope_qc[:].rearrange("p t d -> p (t d)")[:, 192:216].rearrange("p (t c) -> p t c", c=4)
        w_n = rope_qs[:].rearrange("p t d -> p (t d)")[:, 0:48].rearrange("p (t c) -> p t c", c=8)
        w_c = rope_qs[:].rearrange("p t d -> p (t d)")[:, 48:96].rearrange("p (t c) -> p t c", c=8)
        e_g = rope_kc[:].rearrange("p t d -> p (t d)")[:, 0:72].rearrange("p (g t c) -> p g t c", g=3, c=4)
        z_g = rope_kc[:].rearrange("p t d -> p (t d)")[:, 72:144].rearrange("p (g t c) -> p g t c", g=3, c=4)
        small = rope_ks[:].rearrange("p t d -> p (t d)")[:, 0:48].rearrange("p (g t c) -> p g t c", g=2, c=4)

        stats_dram = nc.dram_tensor("stats_scratch", [TOK, 16], F32, kind="Internal").ap()
        weights_dram = nc.dram_tensor("weights_scratch", [TOK, 8], F32, kind="Internal").ap()

        def banks(name):
            return [ctx.enter_context(nc.psum_tensor(f"{name}{i}", [P, 512], F32)) for i in range(2)]

        unit_ps, score_ps, turn_ps, out_ps = banks("unit_ps"), banks("score_ps"), banks("turn_ps"), banks("out_ps")

        raw_in = [sem(f"raw_in{i}") for i in range(RAW)]
        x_landed = [sem(f"x_landed{i}") for i in range(TILES)]
        ident_in = sem("ident_in")
        tables_in = sem("tables_in")
        gain_in = sem("gain_in")
        rope_in = sem("rope_in")
        mlp_gains_in = sem("mlp_gains_in")
        hi_cut = sem("hi_cut")
        lo_cut = sem("lo_cut")
        squares = sem("squares")
        roots = sem("roots")
        xn_ready = sem("xn_ready")
        unit_done = sem("unit_done")
        unit_free = [sem(f"unit_free{i}") for i in range(2)]
        turned = sem("turned")
        turn_hi = sem("turn_hi")
        turn_free = [sem(f"turn_free{i}") for i in range(2)]
        qk_squares = sem("qk_squares")
        qk_roots = sem("qk_roots")
        tok_ready = sem("tok_ready")
        scored = sem("scored")
        even_heads = sem("even_heads")
        maxed = sem("maxed")
        expd = sem("expd")
        out_done = sem("out_done")
        out_read = sem("out_read")
        stats_packed = sem("stats_packed")
        stats_out = sem("stats_out")
        stats_back = sem("stats_back")
        diffs = sem("diffs")
        exps_g = sem("exps_g")
        shares = sem("shares")
        shares_out = sem("shares_out")
        shares_back = sem("shares_back")
        weighted = sem("weighted")
        mixed_done = sem("mixed_done")
        mix_hi = sem("mix_hi")
        mix_ready = sem("mix_ready")
        x2_landed = [sem(f"x2_landed{i}") for i in range(TILES)]
        relu_done = sem("relu_done")
        u_squared = [sem(f"u_squared{i}") for i in range(2)]
        u_ready = sem("u_ready")
        y_ready = sem("y_ready")
        y_out = sem("y_out")
        dve_step = sem("dve_step")
        N_UNITS, N_TURNS, N_CHUNKS, N_BLOCKS = len(plan.unit_no), len(plan.turn_no), len(plan.chunks), len(blocks)
        assert N_UNITS % 2 == 0 and len(units) % 2 == 0 and N_CHUNKS % RAW == 0 and KC == 2 * RAW
        FIRST_SLOT = N_CHUNKS % RING

        def free_of(sems, n):
            return sems[n % 2], n // 2 + 1

        def wait_bank(eng, sems, n):
            if n >= 2:
                eng.wait_ge(sems[n % 2], n // 2)

        def tokens_of(name, t):
            if name in ("v12", "qk1", "qk2"):
                return slice(t, PROMPT, 4) if t < PROMPT_TILES else slice(PROMPT + t - 4, TOK, 2)
            return slice(t * P, (t + 1) * P)

        block = ctx.enter_context(nc.Block())

        @block.sync
        def _(sp):
            sp.dma_start(x_in[:, 0, :], x_rows(0)).then_inc(x_landed[0], 16)
            sp.dma_start(gain_bc[:, :], g_mix[0].partition_broadcast(P)).then_inc(gain_in, 16)

            def load_chunk(n):
                if n >= RAW:
                    sp.wait_ge(lo_cut, n - RAW + 1)
                at = 0
                for matrix, row, col, width in plan.chunks[n]:
                    sp.dma_start(raw[:, n % RAW, at:at + width],
                                 matrices[matrix][row:row + P, col:col + width]).then_inc(raw_in[n % RAW], 16)
                    at += width

            load_chunk(0)
            sp.dma_start(ident[:, :], ident_tab).then_inc(ident_in, 16)
            for t in range(1, TILES):
                sp.dma_start(x_in[:, t, :], x_rows(t)).then_inc(x_landed[t], 16)
                if t < RAW:
                    load_chunk(t)
            sp.dma_start(band_mask[:, :], mask_tab[:, 0:3 * P]).then_inc(tables_in, 16)
            sp.dma_start(class_mask[:, :, :],
                         mask_tab[:, 3 * P:].rearrange("p (m c) -> p m c", m=3)).then_inc(tables_in, 16)
            sp.dma_start(rope_b[:, :, :, :], rope_b_tab).then_inc(tables_in, 16)
            sp.dma_start(rope_raw[:, :, :, :], rope_a_tab).then_inc(rope_in, 16)
            sp.dma_start(qk_gain[:, 0, :], q_gain[0].partition_broadcast(P)).then_inc(rope_in, 16)
            sp.dma_start(qk_gain[:, 1, :], k_gain[0].partition_broadcast(P)).then_inc(rope_in, 16)
            for n in range(RAW, N_CHUNKS):
                load_chunk(n)

            with sp.Fori(0, MLP_STEPS) as i:
                for c in range(2 * KC):
                    n = N_CHUNKS + c
                    sp.wait_ge(lo_cut, i * (2 * KC) + n - RAW + 1)
                    src = w_up[c * P:(c + 1) * P, bass.ds(i * COLS, COLS)] if c < KC else \
                        w_down[bass.ds(i * COLS + (c % 4) * P, P), (c - KC) // 4 * COLS:((c - KC) // 4 + 1) * COLS]
                    sp.dma_start(raw[:, n % RAW, :], src).then_inc(raw_in[n % RAW], 16)
            for t in range(TILES):
                sp.wait_ge(y_ready, t + 1)
                sp.dma_start(y_rows(t), x2[:, t, :]).then_inc(y_out, 16)
            sp.wait_ge(y_out, 16 * TILES)

        @block.gpsimd
        def _(pool):
            def cut_lo(slot, raw_slot):
                pool.tensor_tensor(ring_lo[:, slot, :], raw[:, raw_slot, :], ring_hi[:, slot, :].bitcast(F32),
                                   ALU.subtract).then_inc(lo_cut, 1)

            for n in range(N_CHUNKS):
                pool.wait_ge(hi_cut, n + 1)
                cut_lo(n % RING, n % RAW)
            with pool.Fori(0, MLP_STEPS) as i:
                for c in range(2 * KC):
                    n = N_CHUNKS + c
                    pool.wait_ge(hi_cut, i * (2 * KC) + n + 1)
                    cut_lo(n % RING, n % RAW)

        @block.tensor
        def _(pe):
            def split_product(out, sta, mov, first, last):
                pe.matmul(out, sta[0], mov[0], start=first, stop=False)
                pe.matmul(out, sta[0], mov[1], start=False, stop=False)
                return pe.matmul(out, sta[1], mov[0], start=False, stop=last)

            def ring(slot, cols=slice(0, COLS)):
                return ring_hi[:, slot, cols], ring_lo[:, slot, cols]

            def unit(name, i):
                n = plan.unit_no[("unit", name, i)]
                wait_bank(pe, unit_free, n)
                out = unit_ps[n % 2]
                first_chunk, size = plan.start[name], plan.size[name]
                token_major = name[:2] not in ("ga", "gb", "ya", "yb")
                if name == "qa":
                    pe.wait_ge(*free_of(turn_free, plan.turn_no[("turn", i, 1)]))
                if name == "ya0" and i == 0:
                    for t in (TILES - 2, TILES - 1):
                        pe.wait_ge(*free_of(turn_free, plan.turn_no[("turn_a", t)]))
                if name == "yb0" and i == 0:
                    for c in range(2):
                        pe.wait_ge(*free_of(turn_free, plan.turn_no[("turn_b", 1, c)]))
                if name[:2] == "wo" and i == 0:
                    pe.wait_ge(mix_ready, KC)
                for k in range(size):
                    if i == 0:
                        pe.wait_ge(lo_cut, first_chunk + k + 1)
                    slot = (first_chunk + k) % RING
                    if token_major:
                        cols = tokens_of(name, i)
                        last = split_product(out[:, :], (act_hi[:, k, cols], act_lo[:, k, cols]), ring(slot),
                                             k == 0, k == size - 1)
                    else:
                        c, h = i // 2, i % 2
                        hi, lo = {"g": (act_hi, act_lo), "a": (oTa_hi, oTa_lo),
                                  "b": (oTb_hi, oTb_lo)}[name[0] if name[0] == "g" else name[1]]
                        cols = slice(h * HALF, (h + 1) * HALF)
                        last = split_product(out[:, 0:HALF], ring(slot, slice(c * P, (c + 1) * P)),
                                             (hi[:, k, cols], lo[:, k, cols]), k == 0, k == size - 1)
                return last

            even_count = [0]

            def scores(u):
                branch, t, segs = units[u]
                bank = score_ps[u % 2]
                names = {"A": ["qa", "kva"], "0": ["qk0"], "1": ["qk1"], "2": ["qk2"]}[branch]
                for name in names:
                    for tt in {t} | {seg[1] + seg[2] - 1 for seg in segs}:
                        pe.wait_ge(*free_of(turn_free, plan.turn_no[("turn_qk", name, tt)]))
                order = sorted(range(len(segs)), key=lambda j: (branch != "A" and segs[j][0] % 2, j))
                for x, j in enumerate(order):
                    h, k0, nk = segs[j]
                    at = j * nk * P
                    if x and branch != "A" and h % 2 and not segs[order[x - 1]][0] % 2:
                        last.then_inc(even_heads, 1)
                        even_count[0] += 1
                        pe.wait_ge(even_heads, even_count[0])
                    if branch == "A":
                        kv, i = h // A_GROUP, h % A_GROUP
                        rows = slice(kv * HD, (kv + 1) * HD)
                        q, k = qT_a[rows, i, t * P:(t + 1) * P], kT_a[rows, k0 * P:(k0 + nk) * P]
                    else:
                        rows = slice(h % 2 * HD, (h % 2 + 1) * HD)
                        if branch == "0":
                            q = qkT_0[rows, h // 2, t * P:(t + 1) * P]
                            k = qkT_0[rows, 2 + h // 2, k0 * P:(k0 + nk) * P]
                        else:
                            q = qkT_c[rows, t % 2, h // 2 * P:(h // 2 + 1) * P]
                            k = qkT_c[rows, t % 2, (2 + h // 2) * P:(3 + h // 2) * P]
                    last = pe.matmul(bank[:, at:at + nk * P], q, k, start=True, stop=True)
                last.then_inc(scored, 1)

            def turn_p(u):
                n = plan.turn_no[("turn_p", u)]
                width = sum(seg[2] for seg in units[u][2])
                pe.wait_ge(expd, u + 1)
                wait_bank(pe, turn_free, n)
                for b in range(width):
                    last = pe.transpose(turn_ps[n % 2][:, b * P:(b + 1) * P],
                                        probs[:, u % 2, b * P:(b + 1) * P], ident[:, :])
                last.then_inc(turned, 1)

            def pv(u):
                branch, t, segs = units[u]
                pe.wait_ge(*free_of(turn_free, plan.turn_no[("turn_p", u)]))
                if u >= 2:
                    pe.wait_ge(out_read, u - 1)
                b = 0
                for s, (h, k0, nk) in enumerate(segs):
                    for j in range(nk):
                        if branch == "A":
                            v = v_a[:, k0 + j, h // A_GROUP * HD:(h // A_GROUP + 1) * HD]
                        else:
                            v = v_b[:, k0 + j, int(branch) * GW + h * HD:int(branch) * GW + (h + 1) * HD]
                        last = pe.matmul(out_ps[u % 2][:, s * HD:(s + 1) * HD], probsT[:, u % 2, b * P:(b + 1) * P],
                                         v, start=(j == 0), stop=(j == nk - 1))
                        b += 1
                last.then_inc(out_done, 1)

            for s in steps:
                kind = s[0]
                if kind == "unit":
                    last = unit(s[1], s[2])
                    last.then_inc(unit_done, 1)
                elif kind in ("turn", "turn2"):
                    n, t, half = plan.turn_no[s], s[1], s[2]
                    if n == 0:
                        pe.wait_ge(ident_in, 16)
                    pe.wait_ge(xn_ready, t + 1 + (TILES if kind == "turn2" else 0))
                    wait_bank(pe, turn_free, n)
                    src = xn if kind == "turn" else xn2
                    for c in range(4):
                        last = pe.transpose(turn_ps[n % 2][:, c * P:(c + 1) * P],
                                            src[:, t % 2, (4 * half + c) * P:(4 * half + c + 1) * P], ident[:, :])
                    last.then_inc(turned, 1)
                elif kind == "turn_qk":
                    n = plan.turn_no[s]
                    pe.wait_ge(tok_ready, plan.qk_no[s] + 1)
                    wait_bank(pe, turn_free, n)
                    for c in range(1 if s[1] == "kva" else 4):
                        last = pe.transpose(turn_ps[n % 2][:, c * P:(c + 1) * P],
                                            tok[:, plan.qk_no[s] % 2, c * P:(c + 1) * P], ident[:, :])
                    last.then_inc(turned, 1)
                elif kind == "scores":
                    scores(s[1])
                elif kind == "turn_p":
                    turn_p(s[1])
                elif kind == "pv":
                    pv(s[1])
                elif kind == "turn_a":
                    n, t = plan.turn_no[s], s[1]
                    pe.wait_ge(out_read, len(units))
                    wait_bank(pe, turn_free, n)
                    for c in range(4):
                        last = pe.transpose(turn_ps[n % 2][:, c * P:(c + 1) * P],
                                            o_a[:, t, c * P:(c + 1) * P], ident[:, :])
                    last.then_inc(turned, 1)
                elif kind == "turn_b":
                    n, seq, c = plan.turn_no[s], s[1], s[2]
                    pe.wait_ge(weighted, B_GROUPS)
                    wait_bank(pe, turn_free, n)
                    tiles = range(PROMPT_TILES) if seq == 0 else range(PROMPT_TILES, TILES)
                    stride, bank = len(tiles), turn_ps[n % 2]
                    for g in range(B_GROUPS):
                        for j, t in enumerate(tiles):
                            cols = slice(j * P, (j + 1) * P) if g == 0 else slice(j, stride * P, stride)
                            last = pe.matmul(bank[:, cols], o_b[:, g, t, c * P:(c + 1) * P], ident[:, :],
                                             start=(g == 0 and j == 0), stop=(g == B_GROUPS - 1 and j == stride - 1),
                                             skip_group_check=True)
                    last.then_inc(turned, 1)

            pe.wait_ge(*free_of(turn_free, N_TURNS - 2))
            pe.wait_ge(*free_of(turn_free, N_TURNS - 1))
            with pe.Fori(0, MLP_STEPS) as i:
                for v in range(8):
                    h, c = v // 4, v % 4
                    if v >= 2:
                        pe.wait_ge(u_squared[v % 2], i * 4 + v // 2)
                    for k in range(KC):
                        if v == 0:
                            pe.wait_ge(lo_cut, i * (2 * KC) + N_CHUNKS + k + 1)
                        slot = (FIRST_SLOT + k) % RING
                        cols = slice(h * HALF, (h + 1) * HALF)
                        last = split_product(score_ps[v % 2][:, 0:HALF], ring(slot, slice(c * P, (c + 1) * P)),
                                             (act_hi[:, k, cols], act_lo[:, k, cols]), k == 0, k == KC - 1)
                    last.then_inc(scored, 1)
                for w in range(2 * TILES):
                    j, t = w // TILES, w % TILES
                    pe.wait_ge(unit_free[w % 2], i * TILES + (N_UNITS + w) // 2)
                    pe.wait_ge(u_ready, i * 8 + 4 * (t // 3 + 1))
                    for k in range(4):
                        if t == 0:
                            pe.wait_ge(lo_cut, i * (2 * KC) + N_CHUNKS + KC + 4 * j + k + 1)
                        slot = (FIRST_SLOT + KC + 4 * j + k) % RING
                        cols = slice(t * P, (t + 1) * P)
                        last = split_product(unit_ps[w % 2][:, :], (u_hi[:, k, cols], u_lo[:, k, cols]), ring(slot),
                                             k == 0, k == 3)
                    last.then_inc(unit_done, 1)

        @block.scalar
        def _(act):
            act.wait_ge(dve_step, 1)
            class_at = [u for u, (branch, _, _) in enumerate(units) if branch in "12"]
            class_units = [units[u][:2] for u in class_at]
            band_end = max(u for u, unit in enumerate(units) if unit[0] == "0") + 1

            def cut_hi(slot, raw_slot):
                act.activation(ring_hi[:, slot, :], raw[:, raw_slot, :], ACT.Copy).then_inc(hi_cut, 1)

            def cut_mlp(i, c):
                n = N_CHUNKS + c
                act.wait_ge(raw_in[n % RAW], i * (16 * 2 * KC // RAW) + plan.raw_total[n % RAW] + 16 * (c // RAW + 1))
                cut_hi(n % RING, n % RAW)

            def block_end(b):
                name = blocks[b][0]
                return plan.unit_no[("unit", name, 7 if name[0] in "gy" else TILES - 1)] + 1

            def norm(x_ap, junk, n):
                act.activation(junk, x_ap, ACT.Square, accum_out=ssq[:, n % 2:n % 2 + 1]).then_inc(squares, 1)
                act.wait_ge(squares, n + 1)
                act.activation(rms[:, n % 2:n % 2 + 1], ssq[:, n % 2:n % 2 + 1], ACT.Sqrt, scale=1.0 / D,
                               bias=eps[:, :]).then_inc(roots, 1)

            def take_unit(name, i):
                n = plan.unit_no[("unit", name, i)]
                bank = unit_ps[n % 2]
                if name in ("qa", "kva", "qk0", "qk1", "qk2"):
                    q = plan.qk_no[("turn_qk", name, i)]
                    act.wait_ge(unit_done, n + 1)
                    if q >= 2:
                        before = next(x for x, m in plan.qk_no.items() if m == q - 2)
                        act.wait_ge(turned, plan.turn_no[before] + 1)
                    if name == "qa":
                        act.activation(tok[:, q % 2, :].rearrange("p (g k d) -> p g k d", g=A_GROUP, k=A_KV),
                                       bank[:, :].rearrange("p (k g d) -> p g k d", k=A_KV, g=A_GROUP),
                                       ACT.Copy).then_inc(unit_free[n % 2], 1)
                    elif name == "kva":
                        act.activation(v_a[:, i, :], bank[:, P:2 * P], ACT.Copy)
                        act.activation(v_b[:, i, 0:GW], bank[:, 2 * P:], ACT.Copy)
                        act.activation(tok[:, q % 2, 0:P], bank[:, 0:P], ACT.Copy).then_inc(unit_free[n % 2], 1)
                    else:
                        act.activation(tok[:, q % 2, :], bank[:, :], ACT.Copy).then_inc(unit_free[n % 2], 1)
                    if name in ("qa", "kva"):
                        nh = A_HEADS if name == "qa" else A_KV
                        act.wait_ge(qk_squares, q + 1)
                        act.activation(qk_rms[:, 0:nh], qk_ssq[:, 0:nh], ACT.Sqrt, scale=1.0 / HD,
                                       bias=eps[:, :]).then_inc(qk_roots, 1)
                elif name == "v12":
                    act.wait_ge(unit_done, n + 1)
                    act.activation(v_b[:, i, GW:], bank[:, :], ACT.Copy).then_inc(unit_free[n % 2], 1)
                elif name[0] == "g":
                    order = ["ga0", "gb0", "gb1", "ga1"].index(name)
                    if order == 0:
                        act.wait_ge(scored, band_end)
                    else:
                        act.wait_ge(*free_of(unit_free, plan.unit_no[("unit", ["ya0", "yb0", "yb1"][order - 1], i)]))
                    act.wait_ge(unit_done, n + 1)
                    act.activation(gate[:, i // 2, i % 2 * HALF:(i % 2 + 1) * HALF], bank[:, 0:HALF], ACT.Exp,
                                   scale=-1.0).then_inc(unit_free[n % 2], 1)

            for s in steps:
                kind = s[0]
                if kind == "hi":
                    n = s[1]
                    if n >= RING:
                        act.wait_ge(unit_done, block_end(plan.owner[n - RING]))
                    act.wait_ge(raw_in[n % RAW], plan.raw_count[n])
                    cut_hi(n % RING, n % RAW)
                elif kind == "norm":
                    t = s[1]
                    act.wait_ge(x_landed[t], 16)
                    if t >= 2:
                        act.wait_ge(turned, plan.turn_no[("turn", t - 2, 1)] + 1)
                    norm(x_in[:, t, :], xn[:, t % 2, :], t)
                elif kind == "norm2":
                    t = s[1]
                    act.wait_ge(*free_of(unit_free, plan.unit_no[("unit", "wo1", t)]))
                    if t >= 2:
                        act.wait_ge(turned, plan.turn_no[("turn2", t - 2, 1)] + 1)
                    norm(x2[:, t, :], xn2[:, t % 2, :], TILES + t)
                elif kind in ("turn", "turn2"):
                    n, t, half = plan.turn_no[s], s[1], s[2]
                    act.wait_ge(turned, n + 1)
                    act.activation(act_hi[:, 4 * half:4 * half + 4, t * P:(t + 1) * P],
                                   turn_ps[n % 2][:, :].rearrange("p (c t) -> p c t", c=4),
                                   ACT.Copy).then_inc(turn_hi, 1)
                elif kind == "turn_qk":
                    n, name, t = plan.turn_no[s], s[1], s[2]
                    act.wait_ge(turned, n + 1)
                    if name in ("qk1", "qk2"):
                        order = class_units.index((name[2], t))
                        if order >= 2:
                            act.wait_ge(scored, class_at[order - 2] + 1)
                        dst = qkT_c[:, t % 2, :]
                    elif name == "qa":
                        dst = qT_a[:, :, t * P:(t + 1) * P]
                    elif name == "kva":
                        dst = kT_a[:, t * P:(t + 1) * P]
                    else:
                        dst = qkT_0[:, :, t * P:(t + 1) * P]
                    src = turn_ps[n % 2][:, 0:P] if name == "kva" else turn_ps[n % 2][:, :]
                    if name in ("qa", "qk0"):
                        src = src.rearrange("p (c t) -> p c t", c=4)
                    act.activation(dst, src, ACT.Copy).then_inc(turn_free[n % 2], 1)
                elif kind == "unit":
                    take_unit(s[1], s[2])
                elif kind == "scores":
                    u = s[1]
                    branch, t, segs = units[u]
                    act.wait_ge(maxed, u + 1)
                    if branch == "A" and u >= 2:
                        act.wait_ge(turned, plan.turn_no[("turn_p", u - 2)] + 1)
                    src = score_ps[u % 2] if branch == "A" else probs[:, u % 2, :]
                    at = 0
                    for j, (h, k0, nk) in enumerate(segs):
                        col = stat_col(branch, t, h)
                        last = act.activation(probs[:, u % 2, at:at + nk * P], src[:, at:at + nk * P], ACT.Exp,
                                              bias=neg_max[:, col:col + 1], scale=SCALE if branch == "A" else 1.0,
                                              accum_out=den[:, col:col + 1])
                        at += nk * P
                    last.then_inc(expd, 1)
                elif kind == "turn_p":
                    u, n = s[1], plan.turn_no[s]
                    width = P * sum(seg[2] for seg in units[u][2])
                    act.wait_ge(turned, n + 1)
                    if u >= 2:
                        act.wait_ge(out_done, u - 1)
                    act.activation(probsT[:, u % 2, 0:width], turn_ps[n % 2][:, 0:width],
                                   ACT.Copy).then_inc(turn_free[n % 2], 1)
                elif kind == "turn_a":
                    n, t = plan.turn_no[s], s[1]
                    act.wait_ge(turned, n + 1)
                    act.activation(oTa_hi[:, :, t * P:(t + 1) * P],
                                   turn_ps[n % 2][:, :].rearrange("p (c t) -> p c t", c=4),
                                   ACT.Copy).then_inc(turn_hi, 1)
                elif kind == "turn_b":
                    n, seq, c = plan.turn_no[s], s[1], s[2]
                    first, width = (0, PROMPT) if seq == 0 else (PROMPT, SAMPLE)
                    act.wait_ge(turned, n + 1)
                    act.activation(oTb_hi[:, c, first:first + width], turn_ps[n % 2][:, 0:width],
                                   ACT.Copy).then_inc(turn_hi, 1)
                elif kind == "send_stats":
                    act.wait_ge(stats_packed, 4)
                    act.dma_start(stats_dram[0:PROMPT, :].rearrange("(a r) c -> a r c", r=4),
                                  stats_c[:, 0:4, :]).then_inc(stats_out, 16)
                    act.dma_start(stats_dram[PROMPT:, :].rearrange("(a r) c -> a r c", r=2),
                                  stats_c[:, 4:6, :]).then_inc(stats_out, 16)
                    act.wait_ge(stats_out, 32)
                    act.dma_start(stats_n, stats_dram.rearrange("(t p) c -> p t c", p=P)).then_inc(stats_back, 16)
                elif kind == "combine":
                    act.wait_ge(diffs, 3)
                    act.activation(e_g, e_g, ACT.Exp).then_inc(exps_g, 1)
                    act.wait_ge(shares, 3)
                    act.dma_start(weights_dram.rearrange("(t p) c -> p t c", p=P), w_n).then_inc(shares_out, 16)
                    act.wait_ge(shares_out, 16)
                    act.dma_start(w_c[:, 0:4, :],
                                  weights_dram[0:PROMPT, :].rearrange("(a r) c -> a r c", r=4)).then_inc(shares_back, 16)
                    act.dma_start(w_c[:, 4:6, :],
                                  weights_dram[PROMPT:, :].rearrange("(a r) c -> a r c", r=2)).then_inc(shares_back, 16)
                elif kind == "split_mix":
                    c = s[1]
                    act.wait_ge(mixed_done, 2 * c + 2 if c >= 4 else 8)
                    act.wait_ge(unit_done, block_end(plan.index["ga1"]))
                    act.activation(act_hi[:, c, :], mixed[c // 4][:, c % 4, :], ACT.Copy).then_inc(mix_hi, 1)
                elif kind == "hi_up":
                    act.wait_ge(unit_done, block_end(plan.index["wo0"]))
                    cut_mlp(0, s[1])
                elif kind == "load_x":
                    act.wait_ge(mixed_done, 16)
                    for t in range(TILES):
                        act.dma_start(x2[:, t, :], x_rows(t)).then_inc(x2_landed[t], 16)
                    act.dma_start(gain_mlp[:, :], g_mlp[0].partition_broadcast(P)).then_inc(mlp_gains_in, 16)
                    act.dma_start(gain_fin[:, :], g_final.partition_broadcast(P)).then_inc(mlp_gains_in, 16)

            def relus(i):
                for v in range(8):
                    act.wait_ge(scored, i * 8 + (len(units) + v + 1))
                    act.activation(relu[:, v % 2, :], score_ps[v % 2][:, 0:HALF], ACT.Relu).then_inc(relu_done, 1)
                    cut_mlp(i, KC + v)

            with act.Fori(0, MLP_STEPS - 1) as i:
                relus(i)
                for c in range(KC):
                    cut_mlp(i + 1, c)
            relus(MLP_STEPS - 1)

            for t in range(TILES):
                n = 2 * TILES + t
                act.wait_ge(*free_of(unit_free, N_UNITS + 2 * TILES * (MLP_STEPS - 1) + TILES + t))
                if t >= 2:
                    act.wait_ge(y_ready, t - 1)
                norm(x2[:, t, :], xn2[:, t % 2, :], n)

        @block.vector
        def _(dve):
            chain = [0]

            def link(ins):
                chain[0] += 1
                ins.then_inc(dve_step, 1)
                dve.wait_ge(dve_step, chain[0])

            link(dve.memset(eps[:, :], EPS))
            mix_order = [s[1] for s in steps if s[0] == "split_mix"]

            def normed(n, dst, src, gain):
                dve.wait_ge(roots, n + 1)
                link(dve.reciprocal(rms[:, n % 2:n % 2 + 1], rms[:, n % 2:n % 2 + 1]))
                return dve.scalar_tensor_tensor(dst, src, rms[:, n % 2:n % 2 + 1], gain, ALU.mult, ALU.mult)

            def lo_of_turn(n, hi, lo, src):
                return dve.tensor_tensor(lo, src, hi.bitcast(F32), ALU.subtract)

            def rotate_a(name, t):
                q = plan.qk_no[("turn_qk", name, t)]
                n = plan.unit_no[("unit", name, t)]
                nh = A_HEADS if name == "qa" else A_KV
                width = nh * HD
                buf = tok[:, q % 2, 0:width]
                pos = t % PROMPT_TILES
                cos, sin = (rope_qc, rope_qs) if name == "qa" else (rope_kc, rope_ks)
                dve.wait_ge(*free_of(unit_free, n))
                if q:
                    dve.wait_ge(tok_ready, q)
                link(dve.tensor_tensor(rot[:, 0:width], buf, buf, ALU.mult))
                dve.tensor_reduce(qk_ssq[:, 0:nh], rot[:, 0:width].rearrange("p (h d) -> p h d", d=HD), AX_X,
                                  ALU.add).then_inc(qk_squares, 1)
                dve.wait_ge(qk_roots, q + 1)
                link(dve.reciprocal(qk_rms[:, 0:nh], qk_rms[:, 0:nh]))
                heads = buf.rearrange("p (h d) -> p h d", d=HD)
                link(dve.tensor_tensor(heads, heads, qk_rms[:, 0:nh].unsqueeze(2).broadcast_to([P, nh, HD]), ALU.mult))
                pairs = buf.rearrange("p (h a x e) -> p h a x e", h=nh, a=2, x=2)
                turned_pairs = rot[:, 0:width].rearrange("p (h a x e) -> p h a x e", h=nh, a=2, x=2)
                sines = sin[:, pos, :].rearrange("p (a x e) -> p a x e", a=2, x=2)
                for x in range(2):
                    last = dve.tensor_tensor(turned_pairs[:, :, :, x, :], pairs[:, :, :, 1 - x, :],
                                             sines[:, :, x, :].unsqueeze(1).broadcast_to([P, nh, 2, 16]), ALU.mult)
                link(last)
                link(dve.tensor_tensor(heads, heads, cos[:, pos, :].unsqueeze(1).broadcast_to([P, nh, HD]), ALU.mult))
                dve.tensor_tensor(buf, buf, rot[:, 0:width], ALU.add).then_inc(tok_ready, 1)

            def rotate_b(name, t):
                q = plan.qk_no[("turn_qk", name, t)]
                n = plan.unit_no[("unit", name, t)]
                row = t % PROMPT_TILES if name == "qk0" else 4 + t
                front = tok[:, q % 2, :].rearrange("p (h d) -> p h d", d=HD)[:, :, 0:16]
                other = rot[:, 0:P].rearrange("p (h d) -> p h d", d=16)
                cos = rope_b[:, row, 0, :].unsqueeze(1).broadcast_to([P, 8, 16])
                dve.wait_ge(*free_of(unit_free, n))
                dve.wait_ge(tok_ready, q)
                for x in range(2):
                    last = dve.tensor_tensor(other[:, :, 8 * x:8 * x + 8], front[:, :, 8 - 8 * x:16 - 8 * x],
                                             rope_b[:, row, 1, 8 * x:8 * x + 8].unsqueeze(1)
                                             .broadcast_to([P, 8, 8]), ALU.mult)
                link(last)
                link(dve.tensor_tensor(front, front, cos, ALU.mult))
                dve.tensor_tensor(front, front, other, ALU.add).then_inc(tok_ready, 1)

            def maxima(u):
                branch, t, segs = units[u]
                dve.wait_ge(scored, u + 1)
                ns, width = len(segs), segs[0][2] * P
                col = stat_col(branch, t, segs[0][0])
                cols = neg_max[:, col:col + ns]
                bank = score_ps[u % 2][:, 0:ns * width]
                if branch == "A":
                    link(dve.tensor_reduce(cols, bank.rearrange("p (s w) -> p s w", s=ns), AX_X, ALU.max))
                    dve.tensor_scalar(cols, cols, -SCALE, None, ALU.mult).then_inc(maxed, 1)
                    return
                if u >= 2:
                    dve.wait_ge(turned, plan.turn_no[("turn_p", u - 2)] + 1)
                dst = probs[:, u % 2, 0:ns * width]
                if branch == "0":
                    first = (segs[0][1] - t + 1) * P
                    shape = [P, ns, width]
                    mask = band_mask[:, first:first + width]
                    mask = mask.unsqueeze(1).broadcast_to(shape)
                    view = "p (s w) -> p s w"
                    split = dict(s=ns)
                elif branch == "1" and t < PROMPT_TILES:
                    mask = band_mask[:, P:2 * P].unsqueeze(1).broadcast_to([P, ns, width])
                    view, split = "p (s w) -> p s w", dict(s=ns)
                else:
                    m = {("1", False): 0, ("2", True): 1, ("2", False): 2}[(branch, t < PROMPT_TILES)]
                    mask = class_mask[:, m, :].unsqueeze(1).broadcast_to([P, ns * width // 8, 8])
                    view, split = "p (s w) -> p s w", dict(w=8)
                link(dve.scalar_tensor_tensor(dst.rearrange(view, **split), bank.rearrange(view, **split), SCALE,
                                              mask, ALU.mult, ALU.add))
                link(dve.tensor_reduce(cols, dst.rearrange("p (s w) -> p s w", s=ns), AX_X, ALU.max))
                dve.tensor_scalar(cols, cols, -1.0, None, ALU.mult).then_inc(maxed, 1)

            def take_out(u):
                branch, t, segs = units[u]
                ns, h = len(segs), segs[0][0]
                col = stat_col(branch, t, h)
                src = out_ps[u % 2][:, 0:ns * HD]
                dve.wait_ge(out_done, u + 1)
                if branch == "A":
                    link(dve.reciprocal(den[:, col:col + ns], den[:, col:col + ns]))
                    dve.tensor_tensor(o_a[:, t, h * HD:(h + ns) * HD].rearrange("p (s d) -> p s d", d=HD),
                                      src.rearrange("p (s d) -> p s d", d=HD),
                                      den[:, col:col + ns].unsqueeze(2).broadcast_to([P, ns, HD]),
                                      ALU.mult).then_inc(out_read, 1)
                else:
                    dve.tensor_copy(o_b[:, int(branch), t, h * HD:(h + ns) * HD], src).then_inc(out_read, 1)

            for s in steps:
                kind = s[0]
                if kind in ("norm", "norm2"):
                    t = s[1]
                    if kind == "norm":
                        dve.wait_ge(x_landed[t], 16)
                        dve.wait_ge(gain_in, 16)
                        normed(t, xn[:, t % 2, :], x_in[:, t, :], gain_bc[:, :]).then_inc(xn_ready, 1)
                    else:
                        dve.wait_ge(mlp_gains_in, 32)
                        normed(TILES + t, xn2[:, t % 2, :], x2[:, t, :], gain_mlp[:, :]).then_inc(xn_ready, 1)
                elif kind in ("turn", "turn2"):
                    n, t, half = plan.turn_no[s], s[1], s[2]
                    dve.wait_ge(turn_hi, plan.split_no[s] + 1)
                    at = (slice(None), slice(4 * half, 4 * half + 4), slice(t * P, (t + 1) * P))
                    last = lo_of_turn(n, act_hi[at], act_lo[at],
                                      turn_ps[n % 2][:, :].rearrange("p (c t) -> p c t", c=4))
                    last.then_inc(turn_free[n % 2], 1)
                elif kind == "unit":
                    name, i = s[1], s[2]
                    n = plan.unit_no[s]
                    if name in ("qa", "kva"):
                        if name == "qa" and i == 0:
                            dve.wait_ge(rope_in, 48)
                            for c, sn, j in ((rope_qc, rope_qs, 0), (rope_kc, rope_ks, 1)):
                                gain = qk_gain[:, j, :].unsqueeze(1).broadcast_to([P, PROMPT_TILES, HD])
                                dve.tensor_tensor(c[:, :, :], rope_raw[:, 0, :, :], gain, ALU.mult)
                                other = qk_gain[:, j, :].rearrange("p (a x e) -> p a x e", a=2, x=2)
                                out = sn[:, :, :].rearrange("p t (a x e) -> p t a x e", a=2, x=2)
                                raw_s = rope_raw[:, 1, :, :].rearrange("p t (a x e) -> p t a x e", a=2, x=2)
                                for x in range(2):
                                    last = dve.tensor_tensor(
                                        out[:, :, :, x, :], raw_s[:, :, :, x, :],
                                        other[:, :, 1 - x, :].unsqueeze(1).broadcast_to([P, PROMPT_TILES, 2, 16]),
                                        ALU.mult)
                            link(last)
                        rotate_a(name, i)
                    elif name in ("qk0", "qk1", "qk2"):
                        dve.wait_ge(tables_in, 48)
                        rotate_b(name, i)
                    elif name[0] == "g":
                        part = gate[:, i // 2, i % 2 * HALF:(i % 2 + 1) * HALF]
                        dve.wait_ge(*free_of(unit_free, n))
                        link(dve.tensor_scalar(part, part, 1.0, None, ALU.add))
                        dve.reciprocal(part, part).then_inc(dve_step, 1)
                        chain[0] += 1
                    elif name[0] == "y":
                        c, h = i // 2, i % 2
                        cols = slice(h * HALF, (h + 1) * HALF)
                        into = mixed[int(name[2])][:, c, cols]
                        if i == 0:
                            dve.wait_ge(dve_step, chain[0])
                        dve.wait_ge(unit_done, n + 1)
                        if name in ("ya0", "yb1"):
                            dve.tensor_tensor(into, unit_ps[n % 2][:, 0:HALF], gate[:, c, cols],
                                              ALU.mult).then_inc(unit_free[n % 2], 1)
                        else:
                            part = mix_part[:, i % 2, :]
                            dve.tensor_tensor(part, unit_ps[n % 2][:, 0:HALF], gate[:, c, cols],
                                              ALU.mult).then_inc(unit_free[n % 2], 1)
                            dve.wait_ge(*free_of(unit_free, n))
                            dve.tensor_tensor(into, into, part, ALU.add).then_inc(mixed_done, 1)
                    elif name[:2] == "wo":
                        j = int(name[2])
                        dve.wait_ge(unit_done, n + 1)
                        if j == 0:
                            dve.wait_ge(x2_landed[i], 16)
                        part = x2[:, i, j * COLS:(j + 1) * COLS]
                        dve.tensor_tensor(part, part, unit_ps[n % 2][:, :], ALU.add).then_inc(unit_free[n % 2], 1)
                elif kind == "scores":
                    maxima(s[1])
                elif kind == "pv":
                    take_out(s[1])
                elif kind == "send_stats":
                    dve.wait_ge(expd, len(units))
                    for j, (src, g) in enumerate(((neg_max, 1), (neg_max, 2), (den, 1), (den, 2))):
                        first = STAT_A + g * STAT_B
                        dve.tensor_copy(stats_c[:, :, 4 * j:4 * j + 4],
                                        src[:, first:first + STAT_B].rearrange("p (t h) -> p t h", h=4))\
                           .then_inc(stats_packed, 1)
                elif kind == "turn_a":
                    n, t = plan.turn_no[s], s[1]
                    dve.wait_ge(turn_hi, plan.split_no[s] + 1)
                    at = (slice(None), slice(0, 4), slice(t * P, (t + 1) * P))
                    lo_of_turn(n, oTa_hi[at], oTa_lo[at], turn_ps[n % 2][:, :].rearrange("p (c t) -> p c t", c=4))\
                        .then_inc(turn_free[n % 2], 1)
                elif kind == "turn_b":
                    n, seq, c = plan.turn_no[s], s[1], s[2]
                    first, width = (0, PROMPT) if seq == 0 else (PROMPT, SAMPLE)
                    dve.wait_ge(turn_hi, plan.split_no[s] + 1)
                    at = (slice(None), c, slice(first, first + width))
                    lo_of_turn(n, oTb_hi[at], oTb_lo[at], turn_ps[n % 2][:, 0:width]).then_inc(turn_free[n % 2], 1)
                elif kind == "combine":
                    dve.wait_ge(stats_back, 16)
                    own = slice(STAT_A, STAT_A + STAT_B)
                    m = [neg_max[:, own].rearrange("p (t h) -> p t h", h=4), stats_n[:, :, 0:4], stats_n[:, :, 4:8]]
                    d = [den[:, own].rearrange("p (t h) -> p t h", h=4), stats_n[:, :, 8:12], stats_n[:, :, 12:16]]
                    top, total = small[:, 0], small[:, 1]
                    link(dve.tensor_tensor(top, m[0], m[1], ALU.min))
                    link(dve.tensor_tensor(top, top, m[2], ALU.min))
                    for g in range(B_GROUPS):
                        dve.tensor_tensor(e_g[:, g], top, m[g], ALU.subtract).then_inc(diffs, 1)
                    dve.wait_ge(exps_g, 1)
                    for g in range(B_GROUPS):
                        link(dve.tensor_tensor(z_g[:, g], e_g[:, g], d[g], ALU.mult))
                    link(dve.tensor_tensor(total, z_g[:, 0], z_g[:, 1], ALU.add))
                    link(dve.tensor_tensor(total, total, z_g[:, 2], ALU.add))
                    link(dve.reciprocal(total, total))
                    for g, out in enumerate((w_0, w_n[:, :, 0:4], w_n[:, :, 4:8])):
                        dve.tensor_tensor(out, e_g[:, g], total, ALU.mult).then_inc(shares, 1)
                    dve.wait_ge(shares, 1)
                    for g, share in enumerate((w_0, w_c[:, :, 0:4], w_c[:, :, 4:8])):
                        if g == 1:
                            dve.wait_ge(shares_back, 32)
                        part = o_b[:, g].rearrange("p t (h d) -> p t h d", d=HD)
                        dve.tensor_tensor(part, part, share.unsqueeze(3).broadcast_to([P, TILES, B_HEADS, HD]),
                                          ALU.mult).then_inc(weighted, 1)
                elif kind == "split_mix":
                    c = s[1]
                    dve.wait_ge(mix_hi, mix_order.index(c) + 1)
                    dve.tensor_tensor(act_lo[:, c, :], mixed[c // 4][:, c % 4, :], act_hi[:, c, :].bitcast(F32),
                                      ALU.subtract).then_inc(mix_ready, 1)

            with dve.Fori(0, MLP_STEPS) as i:
                for v in range(8):
                    h, c = v // 4, v % 4
                    cols = slice(h * HALF, (h + 1) * HALF)
                    dve.wait_ge(relu_done, i * 8 + v + 1)
                    dve.scalar_tensor_tensor(usq[:, v % 2, :], score_ps[v % 2][:, 0:HALF], 0.0, relu[:, v % 2, :],
                                             ALU.max, ALU.mult).then_inc(u_squared[v % 2], 1)
                    dve.wait_ge(u_squared[v % 2], i * 4 + v // 2 + 1)
                    dve.tensor_copy(u_hi[:, c, cols], usq[:, v % 2, :]).then_inc(dve_step, 1)
                    dve.wait_ge(dve_step, i * 8 + (chain[0] + v + 1))
                    dve.tensor_tensor(u_lo[:, c, cols], usq[:, v % 2, :], u_hi[:, c, cols].bitcast(F32),
                                      ALU.subtract).then_inc(u_ready, 1)
                for w in range(2 * TILES):
                    j, t = w // TILES, w % TILES
                    dve.wait_ge(unit_done, i * (2 * TILES) + N_UNITS + w + 1)
                    part = x2[:, t, j * COLS:(j + 1) * COLS]
                    dve.tensor_tensor(part, part, unit_ps[w % 2][:, :], ALU.add).then_inc(unit_free[w % 2], 1)
            chain[0] += 8 * MLP_STEPS
            for t in range(TILES):
                normed(2 * TILES + t, x2[:, t, :], x2[:, t, :], gain_fin[:, :]).then_inc(y_ready, 1)


def rope_angles(pos, dim, theta):
    freqs = np.float32(theta) ** (-(np.arange(dim // 2, dtype=np.float32) * np.float32(2.0)) / np.float32(dim))
    return pos.astype(np.float32)[:, None] * freqs[None, :].astype(np.float32)


def shape_tables():
    pos = np.arange(PROMPT)
    row, col = rope_angles(pos // 64, HD // 2, 10000.0), rope_angles(pos % 64, HD // 2, 10000.0)
    cos = np.concatenate([np.cos(row), np.cos(row), np.cos(col), np.cos(col)], 1)
    sin = np.concatenate([-np.sin(row), np.sin(row), -np.sin(col), np.sin(col)], 1)
    a = np.stack([cos, sin]).reshape(2, PROMPT_TILES, P, HD).transpose(2, 0, 1, 3)
    rows = np.arange(P)
    order = [t * P + rows for t in range(4)] + [4 * rows + r for r in range(4)] + [2 * rows + r for r in range(2)]
    b = []
    for p in order:
        ang = rope_angles(p, 16, 500000.0)
        b.append(np.stack([np.concatenate([np.cos(ang), np.cos(ang)], 1),
                           np.concatenate([-np.sin(ang), np.sin(ang)], 1)], 1))
    b = np.stack(b, 1)
    keys = np.arange(3 * P) - P
    band = np.where(np.abs(keys[None, :] - rows[:, None]) <= 64, 0.0, NEG)
    same = [np.where(rows[:, None] % m == np.arange(8)[None, :] % m, 0.0, NEG) for m in (2, 4, 8)]
    mask = np.concatenate([band] + same, 1)
    out = {"rope_a_tab": a, "rope_b_tab": b, "mask_tab": mask, "ident_tab": np.eye(P)}
    return {k: np.ascontiguousarray(v, dtype=np.float32) for k, v in out.items()}


_INS = ["x_prompt", "x_sample", "w_in", "w_a_out", "w_b_out", "w_out", "g_mix", "q_gain", "k_gain", "g_mlp",
        "w_up", "w_down", "g_final"]
_TABLES = ["rope_a_tab", "rope_b_tab", "mask_tab", "ident_tab"]


def kernel(**inputs):
    import concourse.bacc as bacc
    from concourse.bass_utils import run_bass_kernel_spmd

    nc = bacc.Bacc("TRN2", target_bir_lowering=False, num_devices=1)
    arrays, args = {}, []
    tables = shape_tables()
    for name in _INS + _TABLES:
        a = np.ascontiguousarray(inputs[name] if name in inputs else tables[name])
        arrays[f"in_{name}"] = a
        args.append(nc.dram_tensor(f"in_{name}", a.shape, mybir.dt.from_np(a.dtype), kind="ExternalInput").ap())
    for name, n in (("y_prompt", PROMPT), ("y_sample", SAMPLE)):
        args.append(nc.dram_tensor(name, (1, n, D), F32, kind="ExternalOutput").ap())
    build(nc, *args)
    r = run_bass_kernel_spmd(nc, [arrays], core_ids=[0])
    return r.results[0]["y_prompt"], r.results[0]["y_sample"]
```

```python
from contextlib import ExitStack

import numpy as np

import concourse.bass as bass
from concourse import mybir

F32 = mybir.dt.float32
F32R = mybir.dt.float32r
ALU = mybir.AluOpType
ACT = mybir.ActivationFunctionType
AX_X = mybir.AxisListType.X

P = 128
D = 1024
KC = D // P
TILES, PROMPT_TILES = 6, 4
TOK = TILES * P
PROMPT, SAMPLE = 512, 256
HALF = TOK // 2
HD = 64
A_HEADS, A_KV, A_GROUP = 8, 2, 4
B_HEADS, B_GROUPS = 4, 3
FF = 4096
COLS = 512
EPS = 1e-6
SCALE = HD ** -0.5
RING = 16
MLP_STEPS = FF // COLS
NEG = -1.0e30

Q_A, K_A, V_A, Q_B, K_B, V_B, G_A, G_B = 0, 512, 640, 768, 1536, 2304, 3072, 4096
GW = B_HEADS * HD

STAT_A = TILES * A_HEADS
STAT_B = TILES * B_HEADS
STATS = STAT_A + B_GROUPS * STAT_B


def weight_blocks():
    def full(name, matrix, col, rows):
        return (name, [[(matrix, k * P, col, COLS)] for k in range(rows // P)])

    def paired(name, cols):
        return (name, [[("w_in", k * P, c, COLS // len(cols)) for c in cols] for k in range(KC)])

    blocks = [full("qa", "w_in", Q_A, D), paired("kva", [K_A, V_B]), paired("qk0", [Q_B, K_B]),
              full("v12", "w_in", V_B + GW, D), paired("qk1", [Q_B + GW, K_B + GW]),
              paired("qk2", [Q_B + 2 * GW, K_B + 2 * GW])]
    gate_a = [full(f"ga{j}", "w_in", G_A + j * COLS, D) for j in range(2)]
    gate_b = [full(f"gb{j}", "w_in", G_B + j * COLS, D) for j in range(2)]
    out_a = [full(f"ya{j}", "w_a_out", j * COLS, A_HEADS * HD) for j in range(2)]
    out_b = [full(f"yb{j}", "w_b_out", j * COLS, B_HEADS * HD) for j in range(2)]
    blocks += [gate_a[0], out_a[0], gate_b[0], out_b[0], gate_b[1], out_b[1], gate_a[1], out_a[1]]
    blocks += [full(f"wo{j}", "w_out", j * COLS, D) for j in range(2)]
    return blocks


def attention_units():
    branch_a, band, classes = [], [], []
    for t in range(PROMPT_TILES):
        branch_a += [("A", t, [(h, 0, 4)]) for h in range(A_HEADS)]
    for t in range(PROMPT_TILES, TILES):
        branch_a += [("A", t, [(h, 4, 2), (h + 1, 4, 2)]) for h in range(0, A_HEADS, 2)]
    for t in range(PROMPT_TILES):
        lo, hi = max(0, t - 1), min(PROMPT_TILES - 1, t + 1)
        band += [("0", t, [(h, lo, hi - lo + 1)]) for h in range(B_HEADS)]
    for t in range(PROMPT_TILES, TILES):
        band += [("0", t, [(h, 4, 2), (h + 1, 4, 2)]) for h in range(0, B_HEADS, 2)]
    for g in "12":
        classes += [(g, t, [(h, t, 1) for h in range(B_HEADS)]) for t in range(TILES)]
    return branch_a, band, classes


def make_schedule():
    blocks = weight_blocks()
    sizes = {name: len(chunks) for name, chunks in blocks}
    owner = [name for name, chunks in blocks for _ in chunks]
    branch_a, band, classes = attention_units()
    steps, units, finished, turned, fresh = [], [], set(), set(), []
    state = {"cut": 0, "tick": 0}

    def cuts(limit):
        for _ in range(limit):
            n = state["cut"]
            if n < len(owner) and (n < RING or owner[n - RING] in finished):
                steps.append(("hi", n))
                state["cut"] += 1

    def unit(name, i, count, rate=0):
        need = len(owner) - owner[::-1].index(name)
        cuts(max(0, need - state["cut"]))
        assert state["cut"] >= need
        for j in range(rate - 1):
            steps.append(("part", name, i, sizes[name] * j // rate, sizes[name] * (j + 1) // rate))
            attend(1)
        steps.append(("unit", name, i))
        if i == count - 1:
            finished.add(name)
        cuts(2)

    def next_unit():
        if branch_a:
            last_keys = branch_a[0][2][0][1] + branch_a[0][2][0][2] - 1
            return branch_a.pop(0) if ("kva", last_keys) in turned else None
        if classes and ("qk" + classes[0][0], classes[0][1]) in turned:
            return classes.pop(0)
        if band and ("qk0", TILES - 1) in turned:
            return band.pop(0)
        return None

    def attend(count):
        for _ in range(count):
            if branch_a or band or classes:
                new = next_unit()
                if new is None:
                    return
                units.append(new)
            i = state["tick"]
            early = i < len(units) and units[i][0] != "A" and units[i - 2][0] != "A"
            if early:
                steps.append(("scores", i))
            if 0 <= i - 2 < len(units):
                steps.append(("turn_p", i - 2))
            if i < len(units) and not early:
                steps.append(("scores", i))
            if 0 <= i - 3 < len(units):
                steps.append(("pv", i - 3))
            state["tick"] += 1

    waiting = []

    def turn_next():
        b, t = waiting.pop(0)
        steps.append(("turn_qk", b, t))
        fresh.append((b, t))

    def rotated_unit(name, t, rate=0):
        unit(name, t, TILES, rate)
        waiting.append((name, t))
        while len(waiting) > 2:
            turn_next()

    steps.append(("norm", 0))
    cuts(2)
    steps += [("turn", 0, 0), ("turn", 0, 1), ("norm", 1)]
    cuts(1)
    steps.append(("part", "qa", 0, 0, 2))
    cuts(1)
    steps += [("turn", 1, 0), ("turn", 1, 1), ("part", "qa", 1, 0, 2)]
    for k in range(2, KC - 1):
        cuts(1)
        steps += [("part", "qa", t, k, k + 1) for t in range(2)]
        if k in (3, 5):
            steps.append(("norm", (k + 1) // 2))
    steps += [("turn", 2, 0), ("turn", 2, 1)]
    rotated_unit("qa", 0)
    for t in range(3, TILES):
        if t + 1 < TILES:
            steps.append(("norm", t + 1))
        steps += [("turn", t, 0), ("turn", t, 1)]
        rotated_unit("qa", t - 2)
    rotated_unit("qa", TILES - 2)
    rotated_unit("qa", TILES - 1)
    for name, rate in (("kva", 3), ("qk0", 3), ("v12", 3), ("qk1", 3), ("qk2", 3)):
        for t in range(TILES):
            if name == "v12":
                unit(name, t, TILES, rate)
                if waiting:
                    turn_next()
            else:
                rotated_unit(name, t, rate)
            attend(1)
            turned.update(fresh)
            fresh.clear()
    while waiting:
        turn_next()
        attend(1)
        turned.update(fresh)
        fresh.clear()
    while band:
        attend(1)
    left = iter(range(TILES))

    def attend_or_turn():
        if state["tick"] < len(units) + 3:
            attend(1)
            if state["tick"] == len(units) + 3:
                steps.append(("send_stats",))
        else:
            t = next(left, None)
            if t is not None:
                steps.append(("turn_a", t))

    for i in range(8):
        unit("ga0", i, 8, 2 if state["tick"] < len(units) + 3 else 0)
        attend_or_turn()
        if i in (5, 6):
            attend_or_turn()
    assert not list(left)
    for i in range(8):
        unit("ya0", i, 8)
        if i == 0:
            steps.append(("fetch_stats",))
        if i == 2:
            steps.append(("combine",))
        if i == 6:
            steps.append(("fetch_shares",))
    turns = [("turn_b", s, c) for s in range(2) for c in range(2)]
    for i in range(8):
        unit("gb0", i, 8)
        if i == 0:
            steps.append(("weight",))
        if i in (3, 4, 5, 6):
            steps.append(turns.pop(0))
    for name in ("yb0", "gb1", "yb1", "ga1"):
        for i in range(8):
            unit(name, i, 8)
    after = {0: [0], 1: [1], 2: [2, 4], 3: [3], 4: [5], 5: [6], 7: [7]}
    for i in range(8):
        unit("ya1", i, 8)
        steps += [("split_mix", c) for c in after.get(i, [])]
    steps.append(("load_x",))
    for i in range(TILES):
        unit("wo0", i, TILES)
    for i in range(TILES):
        unit("wo1", i, TILES)
        steps.append(("norm2", i))
        if i < 4:
            steps += [("hi_up", 2 * i), ("hi_up", 2 * i + 1)]
        if i >= 2:
            steps += [("turn2", i - 2, 0), ("turn2", i - 2, 1)]
    steps += [("turn2", t, half) for t in (TILES - 2, TILES - 1) for half in range(2)]
    assert state["cut"] == len(owner) and not (branch_a or band or classes)
    return blocks, units, steps


class Plan:

    def __init__(self):
        self.blocks, self.units, self.steps = make_schedule()
        self.chunks = [c for _, chunks in self.blocks for c in chunks]
        self.start, self.index, self.size = {}, {}, {}
        n = 0
        for b, (name, chunks) in enumerate(self.blocks):
            self.start[name], self.index[name], self.size[name] = n, b, len(chunks)
            n += len(chunks)
        self.owner = [b for b, (_, chunks) in enumerate(self.blocks) for _ in chunks]
        self.unit_no, self.turn_no, self.qk_no = {}, {}, {}
        self.split_no = {}
        for s in self.steps:
            if s[0] == "unit":
                self.unit_no[s] = len(self.unit_no)
            elif s[0] in ("turn", "turn_qk", "turn_p", "turn_a", "turn_b", "turn2"):
                self.turn_no[s] = len(self.turn_no)
                if s[0] == "turn_qk":
                    self.qk_no[s] = len(self.qk_no)
                elif s[0] != "turn_p":
                    self.split_no[s] = len(self.split_no)
        self.landed, self.landed_total = [], [0] * RING
        for n, c in enumerate(self.chunks):
            self.landed_total[n % RING] += 16 * len(c)
            self.landed.append(self.landed_total[n % RING])


def stat_col(branch, t, h):
    return t * A_HEADS + h if branch == "A" else STAT_A + int(branch) * STAT_B + t * B_HEADS + h


def build(nc, x_prompt, x_sample, w_in, w_a_out, w_b_out, w_out, g_mix, q_gain, k_gain, g_mlp, w_up,
          w_down, g_final, rope_a_tab, rope_b_tab, mask_tab, ident_tab, y_prompt, y_sample):
    plan = Plan()
    blocks, units, steps = plan.blocks, plan.units, plan.steps
    matrices = {"w_in": w_in[0], "w_a_out": w_a_out[0], "w_b_out": w_b_out[0], "w_out": w_out[0]}
    w_up, w_down = w_up[0], w_down[0]

    def x_rows(t):
        return x_prompt[0, t * P:(t + 1) * P, :] if t < PROMPT_TILES \
            else x_sample[0, (t - PROMPT_TILES) * P:(t - PROMPT_TILES + 1) * P, :]

    def y_rows(t):
        return y_prompt[0, t * P:(t + 1) * P, :] if t < PROMPT_TILES \
            else y_sample[0, (t - PROMPT_TILES) * P:(t - PROMPT_TILES + 1) * P, :]

    with ExitStack() as ctx:
        def sb(stack, name, shape, dt=F32):
            return stack.enter_context(nc.sbuf_tensor(name, shape, dt))

        def sem(name):
            return ctx.enter_context(nc.semaphore(name))

        st = ExitStack()
        ring_whole = sb(st, "ring_whole", [P, RING, COLS])
        st.close()
        ring_lo = sb(ctx, "ring_lo", [P, RING, COLS], F32R)
        ring_hi = sb(ctx, "ring_hi", [P, RING, COLS], F32R)
        act_hi = sb(ctx, "act_hi", [P, KC, TOK], F32R)
        act_lo = sb(ctx, "act_lo", [P, KC, TOK], F32R)
        ident = sb(ctx, "ident", [P, P])
        band_mask = sb(ctx, "band_mask", [P, 3 * P])
        class_mask = sb(ctx, "class_mask", [P, 3, 8])
        rope_qc = sb(ctx, "rope_qc", [P, PROMPT_TILES, HD])
        rope_qs = sb(ctx, "rope_qs", [P, PROMPT_TILES, HD])
        rope_kc = sb(ctx, "rope_kc", [P, PROMPT_TILES, HD])
        rope_ks = sb(ctx, "rope_ks", [P, PROMPT_TILES, HD])
        rope_b = sb(ctx, "rope_b", [P, 10, 2, 16])
        neg_max = sb(ctx, "neg_max", [P, STATS])
        den = sb(ctx, "den", [P, STATS])
        eps = sb(ctx, "eps", [P, 1])
        ssq = sb(ctx, "ssq", [P, 2])
        rms = sb(ctx, "rms", [P, 2])
        qk_ssq = sb(ctx, "qk_ssq", [P, 8])
        qk_rms = sb(ctx, "qk_rms", [P, 8])

        st = ExitStack()
        x_in = sb(st, "x_in", [P, TILES, D])
        gain_bc = sb(st, "gain_bc", [P, D])
        xn = sb(st, "xn", [P, 2, D])
        st.close()

        st = ExitStack()
        qT_a = sb(st, "qT_a", [P, 4, TOK])
        kT_a = sb(st, "kT_a", [P, A_KV, TOK])
        v_a = sb(st, "v_a", [P, TILES, A_KV * HD])
        o_a = sb(st, "o_a", [P, TILES, A_HEADS * HD])
        probs = sb(st, "probs", [P, 2, 512])
        probsT = sb(st, "probsT", [P, 2, 512])
        tok = sb(st, "tok", [P, 2, 512])
        rot = sb(st, "rot", [P, 512])
        qkT_c = sb(st, "qkT_c", [P, 2, 512])
        v_b = sb(st, "v_b", [P, TILES, B_GROUPS * GW])
        qkT_0 = sb(st, "qkT_0", [P, 4, TOK])
        st.close()
        st = ExitStack()
        sb(st, "hold_r", [P, 52224 // 4])
        rope_raw = sb(st, "rope_raw", [P, 2, PROMPT_TILES, HD])
        qk_gain = sb(st, "qk_gain", [P, 2, HD])
        st.close()

        st = ExitStack()
        o_b = sb(st, "o_b", [P, B_GROUPS, TILES, GW])
        st.close()
        st = ExitStack()
        sb(st, "hold_o", [P, (21504 + 12288) // 4])
        oTa_hi = sb(st, "oTa_hi", [P, 4, TOK], F32R)
        oTa_lo = sb(st, "oTa_lo", [P, 4, TOK], F32R)
        oTb_hi = sb(st, "oTb_hi", [P, 2, TOK], F32R)
        oTb_lo = sb(st, "oTb_lo", [P, 2, TOK], F32R)
        gate = sb(st, "gate", [P, 4, TOK])
        st.close()
        st = ExitStack()
        mixed_1 = sb(st, "mixed_1", [P, 4, TOK])
        mix_part = sb(st, "mix_part", [P, 2, HALF])
        sb(st, "hold_m", [P, 6144 // 4])
        mixed_0 = sb(st, "mixed_0", [P, 4, TOK])
        st.close()
        mixed = (mixed_0, mixed_1)

        st = ExitStack()
        u_hi = sb(st, "u_hi", [P, 4, TOK], F32R)
        u_lo = sb(st, "u_lo", [P, 4, TOK], F32R)
        relu = sb(st, "relu", [P, 2, HALF])
        usq = sb(st, "usq", [P, 2, HALF])
        sb(st, "hold_x", [P, 3072 // 4])
        x2 = sb(st, "x2", [P, TILES, D])
        gain_mlp = sb(st, "gain_mlp", [P, D])
        gain_fin = sb(st, "gain_fin", [P, D])
        xn2 = sb(st, "xn2", [P, 2, D])
        st.close()

        stats_c = rope_qc[:].rearrange("p t d -> p (t d)")[:, 0:96].rearrange("p (t c) -> p t c", c=16)
        stats_n = rope_qc[:].rearrange("p t d -> p (t d)")[:, 96:192].rearrange("p (t c) -> p t c", c=16)
        w_0 = rope_qc[:].rearrange("p t d -> p (t d)")[:, 192:216].rearrange("p (t c) -> p t c", c=4)
        w_n = rope_qs[:].rearrange("p t d -> p (t d)")[:, 0:48].rearrange("p (t c) -> p t c", c=8)
        w_c = rope_qs[:].rearrange("p t d -> p (t d)")[:, 48:96].rearrange("p (t c) -> p t c", c=8)
        e_g = rope_kc[:].rearrange("p t d -> p (t d)")[:, 0:72].rearrange("p (g t c) -> p g t c", g=3, c=4)
        z_g = rope_kc[:].rearrange("p t d -> p (t d)")[:, 72:144].rearrange("p (g t c) -> p g t c", g=3, c=4)
        small = rope_ks[:].rearrange("p t d -> p (t d)")[:, 0:48].rearrange("p (g t c) -> p g t c", g=2, c=4)

        stats_dram = nc.dram_tensor("stats_scratch", [TOK, 16], F32, kind="Internal").ap()
        weights_dram = nc.dram_tensor("weights_scratch", [TOK, 8], F32, kind="Internal").ap()

        def banks(name):
            return [ctx.enter_context(nc.psum_tensor(f"{name}{i}", [P, 512], F32)) for i in range(2)]

        unit_ps, score_ps, turn_ps, out_ps = banks("unit_ps"), banks("score_ps"), banks("turn_ps"), banks("out_ps")

        landed = [sem(f"landed{i}") for i in range(RING)]
        x_landed = [sem(f"x_landed{i}") for i in range(TILES)]
        ident_in = sem("ident_in")
        tables_in = sem("tables_in")
        gain_in = sem("gain_in")
        rope_in = sem("rope_in")
        mlp_gains_in = sem("mlp_gains_in")
        hi_cut = sem("hi_cut")
        lo_cut = sem("lo_cut")
        squares = sem("squares")
        roots = sem("roots")
        xn_ready = sem("xn_ready")
        unit_done = sem("unit_done")
        unit_free = [sem(f"unit_free{i}") for i in range(2)]
        turned = sem("turned")
        turn_hi = sem("turn_hi")
        turn_free = [sem(f"turn_free{i}") for i in range(2)]
        qk_squares = sem("qk_squares")
        qk_roots = sem("qk_roots")
        tok_ready = sem("tok_ready")
        scored = sem("scored")
        even_heads = sem("even_heads")
        maxed = sem("maxed")
        expd = sem("expd")
        out_done = sem("out_done")
        out_read = sem("out_read")
        stats_packed = sem("stats_packed")
        stats_out = sem("stats_out")
        stats_back = sem("stats_back")
        diffs = sem("diffs")
        exps_g = sem("exps_g")
        shares = sem("shares")
        shares_out = sem("shares_out")
        shares_back = sem("shares_back")
        weighted = sem("weighted")
        mixed_done = sem("mixed_done")
        mix_hi = sem("mix_hi")
        mix_ready_0 = sem("mix_ready_0")
        mix_ready_1 = sem("mix_ready_1")
        x2_landed = [sem(f"x2_landed{i}") for i in range(TILES)]
        relu_done = sem("relu_done")
        u_squared = [sem(f"u_squared{i}") for i in range(2)]
        u_ready = sem("u_ready")
        y_ready = sem("y_ready")
        y_out = sem("y_out")
        dve_step = sem("dve_step")
        N_UNITS, N_TURNS, N_CHUNKS, N_BLOCKS = len(plan.unit_no), len(plan.turn_no), len(plan.chunks), len(blocks)
        assert N_UNITS % 2 == 0 and len(units) % 2 == 0
        FIRST_SLOT = N_CHUNKS % RING
        assert RING == 2 * KC

        def free_of(sems, n):
            return sems[n % 2], n // 2 + 1

        def wait_bank(eng, sems, n):
            if n >= 2:
                eng.wait_ge(sems[n % 2], n // 2)

        def tokens_of(name, t):
            if name in ("v12", "qk1", "qk2"):
                return slice(t, PROMPT, 4) if t < PROMPT_TILES else slice(PROMPT + t - 4, TOK, 2)
            return slice(t * P, (t + 1) * P)

        def block_end(b):
            name = blocks[b][0]
            return plan.unit_no[("unit", name, 7 if name[0] in "gy" else TILES - 1)] + 1

        mix_order = [s[1] for s in steps if s[0] == "split_mix"]

        block = ctx.enter_context(nc.Block())

        @block.sync
        def _(sp):
            def load_chunks(ns):
                for n in ns:
                    if n >= RING:
                        sp.wait_ge(unit_done, block_end(plan.owner[n - RING]))
                    at = 0
                    for matrix, row, col, width in plan.chunks[n]:
                        sp.dma_start(ring_whole[:, n % RING, at:at + width],
                                     matrices[matrix][row:row + P, col:col + width]).then_inc(landed[n % RING], 16)
                        at += width

            def load_x(t):
                sp.dma_start(x_in[:, t, :], x_rows(t)).then_inc(x_landed[t], 16)

            load_x(0)
            sp.dma_start(gain_bc[:, :], g_mix[0].partition_broadcast(P)).then_inc(gain_in, 16)
            sp.dma_start(ident[:, :], ident_tab).then_inc(ident_in, 16)
            load_chunks((0, 1))
            load_x(1)
            load_chunks(range(2, KC))
            load_x(2)
            sp.dma_start(rope_raw[:, :, :, :], rope_a_tab).then_inc(rope_in, 16)
            sp.dma_start(qk_gain[:, 0, :], q_gain[0].partition_broadcast(P)).then_inc(rope_in, 16)
            sp.dma_start(qk_gain[:, 1, :], k_gain[0].partition_broadcast(P)).then_inc(rope_in, 16)
            for t in range(3, TILES):
                load_x(t)
            load_chunks(range(KC, 2 * KC))
            sp.dma_start(band_mask[:, :], mask_tab[:, 0:3 * P]).then_inc(tables_in, 16)
            sp.dma_start(class_mask[:, :, :],
                         mask_tab[:, 3 * P:].rearrange("p (m c) -> p m c", m=3)).then_inc(tables_in, 16)
            sp.dma_start(rope_b[:, :, :, :], rope_b_tab).then_inc(tables_in, 16)
            load_chunks(range(2 * KC, N_CHUNKS))

            sp.wait_ge(unit_done, block_end(plan.index["wo0"]))
            with sp.Fori(0, MLP_STEPS) as i:
                for c in range(2 * KC):
                    if c == 0:
                        sp.wait_ge(scored, i * 8 + len(units))
                    if c == KC:
                        sp.wait_ge(unit_done, i * (2 * TILES) + N_UNITS)
                    src = w_up[c * P:(c + 1) * P, bass.ds(i * COLS, COLS)] if c < KC else \
                        w_down[bass.ds(i * COLS + (c % 4) * P, P), (c - KC) // 4 * COLS:((c - KC) // 4 + 1) * COLS]
                    slot = (N_CHUNKS + c) % RING
                    sp.dma_start(ring_whole[:, slot, :], src).then_inc(landed[slot], 16)
            for t in range(TILES):
                sp.wait_ge(y_ready, t + 1)
                sp.dma_start(y_rows(t), x2[:, t, :]).then_inc(y_out, 16)
            sp.wait_ge(y_out, 16 * TILES)

        @block.gpsimd
        def _(pool):
            def cut_lo(slot):
                pool.tensor_tensor(ring_lo[:, slot, :], ring_whole[:, slot, :], ring_hi[:, slot, :].bitcast(F32),
                                   ALU.subtract).then_inc(lo_cut, 1)

            for s in steps:
                if s[0] == "hi":
                    n = s[1]
                    pool.wait_ge(hi_cut, n + 1)
                    cut_lo(n % RING)
                elif s[0] == "split_mix" and s[1] < 4:
                    c = s[1]
                    pool.wait_ge(mix_hi, mix_order.index(c) + 1)
                    pool.tensor_tensor(act_lo[:, c, :], mixed_0[:, c, :], act_hi[:, c, :].bitcast(F32),
                                       ALU.subtract).then_inc(mix_ready_0, 1)
            with pool.Fori(0, MLP_STEPS) as i:
                for c in range(2 * KC):
                    n = N_CHUNKS + c
                    pool.wait_ge(hi_cut, i * (2 * KC) + n + 1)
                    cut_lo(n % RING)

        @block.tensor
        def _(pe):
            def split_product(out, sta, mov, first, last):
                pe.matmul(out, sta[0], mov[0], start=first, stop=False)
                pe.matmul(out, sta[0], mov[1], start=False, stop=False)
                return pe.matmul(out, sta[1], mov[0], start=False, stop=last)

            def ring(slot, cols=slice(0, COLS)):
                return ring_hi[:, slot, cols], ring_lo[:, slot, cols]

            begun = {}

            def unit(name, i, end):
                n = plan.unit_no[("unit", name, i)]
                begin = begun.get(n, 0)
                begun[n] = end
                if begin == 0:
                    wait_bank(pe, unit_free, n)
                out = unit_ps[n % 2]
                first_chunk, size = plan.start[name], plan.size[name]
                token_major = name[:2] not in ("ga", "gb", "ya", "yb")
                if name == "qa" and begin == 0:
                    pe.wait_ge(*free_of(turn_free, plan.turn_no[("turn", i, 1)]))
                if name == "ya0" and i == 0:
                    for t in (TILES - 2, TILES - 1):
                        pe.wait_ge(*free_of(turn_free, plan.turn_no[("turn_a", t)]))
                if name == "yb0" and i == 0:
                    for c in range(2):
                        pe.wait_ge(*free_of(turn_free, plan.turn_no[("turn_b", 1, c)]))
                for k in range(begin, end):
                    if i == 0:
                        pe.wait_ge(lo_cut, first_chunk + k + 1)
                    if name == "wo0" and i == 0:
                        pe.wait_ge(*((mix_ready_0, k + 1) if k < 4 else (mix_ready_1, k - 3)))
                    slot = (first_chunk + k) % RING
                    if token_major:
                        cols = tokens_of(name, i)
                        last = split_product(out[:, :], (act_hi[:, k, cols], act_lo[:, k, cols]), ring(slot),
                                             k == 0, k == size - 1)
                    else:
                        c, h = i // 2, i % 2
                        hi, lo = {"g": (act_hi, act_lo), "a": (oTa_hi, oTa_lo),
                                  "b": (oTb_hi, oTb_lo)}[name[0] if name[0] == "g" else name[1]]
                        cols = slice(h * HALF, (h + 1) * HALF)
                        last = split_product(out[:, 0:HALF], ring(slot, slice(c * P, (c + 1) * P)),
                                             (hi[:, k, cols], lo[:, k, cols]), k == 0, k == size - 1)
                return last

            even_count = [0]

            def scores(u):
                branch, t, segs = units[u]
                if branch != "A" and units[u - 2][0] != "A":
                    pe.wait_ge(maxed, u - 1)
                bank = score_ps[u % 2]
                names = {"A": ["qa", "kva"], "0": ["qk0"], "1": ["qk1"], "2": ["qk2"]}[branch]
                for name in names:
                    for tt in {t} | {seg[1] + seg[2] - 1 for seg in segs}:
                        pe.wait_ge(*free_of(turn_free, plan.turn_no[("turn_qk", name, tt)]))
                order = sorted(range(len(segs)), key=lambda j: (branch != "A" and segs[j][0] % 2, j))
                for x, j in enumerate(order):
                    h, k0, nk = segs[j]
                    at = j * nk * P
                    if x and branch != "A" and h % 2 and not segs[order[x - 1]][0] % 2:
                        last.then_inc(even_heads, 1)
                        even_count[0] += 1
                        pe.wait_ge(even_heads, even_count[0])
                    if branch == "A":
                        kv, i = h // A_GROUP, h % A_GROUP
                        q, k = qT_a[:, i, t * P:(t + 1) * P], kT_a[:, kv, k0 * P:(k0 + nk) * P]
                    else:
                        rows = slice(h % 2 * HD, (h % 2 + 1) * HD)
                        if branch == "0":
                            q = qkT_0[rows, h // 2, t * P:(t + 1) * P]
                            k = qkT_0[rows, 2 + h // 2, k0 * P:(k0 + nk) * P]
                        else:
                            q = qkT_c[rows, t % 2, h // 2 * P:(h // 2 + 1) * P]
                            k = qkT_c[rows, t % 2, (2 + h // 2) * P:(3 + h // 2) * P]
                    last = pe.matmul(bank[:, at:at + nk * P], q, k, start=True, stop=True)
                last.then_inc(scored, 1)

            def turn_p(u):
                n = plan.turn_no[("turn_p", u)]
                width = sum(seg[2] for seg in units[u][2])
                pe.wait_ge(expd, u + 1)
                wait_bank(pe, turn_free, n)
                for b in range(width):
                    last = pe.transpose(turn_ps[n % 2][:, b * P:(b + 1) * P],
                                        probs[:, u % 2, b * P:(b + 1) * P], ident[:, :])
                last.then_inc(turned, 1)

            def pv(u):
                branch, t, segs = units[u]
                pe.wait_ge(*free_of(turn_free, plan.turn_no[("turn_p", u)]))
                if u >= 2:
                    pe.wait_ge(out_read, u - 1)
                b = 0
                for s, (h, k0, nk) in enumerate(segs):
                    for j in range(nk):
                        if branch == "A":
                            v = v_a[:, k0 + j, :]
                        else:
                            first = int(branch) * GW + h // 2 * P
                            v = v_b[:, k0 + j, first:first + P]
                        last = pe.matmul(out_ps[u % 2][:, s * P:(s + 1) * P], probsT[:, u % 2, b * P:(b + 1) * P],
                                         v, start=(j == 0), stop=(j == nk - 1))
                        b += 1
                last.then_inc(out_done, 1)

            for s in steps:
                kind = s[0]
                if kind == "unit":
                    unit(s[1], s[2], plan.size[s[1]]).then_inc(unit_done, 1)
                elif kind == "part":
                    unit(s[1], s[2], s[4])
                elif kind in ("turn", "turn2"):
                    n, t, half = plan.turn_no[s], s[1], s[2]
                    if n == 0:
                        pe.wait_ge(ident_in, 16)
                    pe.wait_ge(xn_ready, t + 1 + (TILES if kind == "turn2" else 0))
                    wait_bank(pe, turn_free, n)
                    src = xn if kind == "turn" else xn2
                    for c in range(4):
                        last = pe.transpose(turn_ps[n % 2][:, c * P:(c + 1) * P],
                                            src[:, t % 2, (4 * half + c) * P:(4 * half + c + 1) * P], ident[:, :])
                    last.then_inc(turned, 1)
                elif kind == "turn_qk":
                    n = plan.turn_no[s]
                    pe.wait_ge(tok_ready, plan.qk_no[s] + 1)
                    wait_bank(pe, turn_free, n)
                    for c in range(1 if s[1] == "kva" else 4):
                        last = pe.transpose(turn_ps[n % 2][:, c * P:(c + 1) * P],
                                            tok[:, plan.qk_no[s] % 2, c * P:(c + 1) * P], ident[:, :])
                    last.then_inc(turned, 1)
                elif kind == "scores":
                    scores(s[1])
                elif kind == "turn_p":
                    turn_p(s[1])
                elif kind == "pv":
                    pv(s[1])
                elif kind == "turn_a":
                    n, t = plan.turn_no[s], s[1]
                    pe.wait_ge(out_read, len(units))
                    wait_bank(pe, turn_free, n)
                    for c in range(4):
                        last = pe.transpose(turn_ps[n % 2][:, c * P:(c + 1) * P],
                                            o_a[:, t, c * P:(c + 1) * P], ident[:, :])
                    last.then_inc(turned, 1)
                elif kind == "turn_b":
                    n, seq, c = plan.turn_no[s], s[1], s[2]
                    pe.wait_ge(weighted, B_GROUPS)
                    wait_bank(pe, turn_free, n)
                    tiles = range(PROMPT_TILES) if seq == 0 else range(PROMPT_TILES, TILES)
                    stride, bank = len(tiles), turn_ps[n % 2]
                    for g in range(B_GROUPS):
                        for j, t in enumerate(tiles):
                            cols = slice(j * P, (j + 1) * P) if g == 0 else slice(j, stride * P, stride)
                            last = pe.matmul(bank[:, cols], o_b[:, g, t, c * P:(c + 1) * P], ident[:, :],
                                             start=(g == 0 and j == 0), stop=(g == B_GROUPS - 1 and j == stride - 1),
                                             skip_group_check=True)
                    last.then_inc(turned, 1)

            pe.wait_ge(*free_of(turn_free, N_TURNS - 2))
            pe.wait_ge(*free_of(turn_free, N_TURNS - 1))
            with pe.Fori(0, MLP_STEPS) as i:
                for v in range(8):
                    h, c = v // 4, v % 4
                    if v >= 2:
                        pe.wait_ge(u_squared[v % 2], i * 4 + v // 2)
                    for k in range(KC):
                        if v == 0:
                            pe.wait_ge(lo_cut, i * (2 * KC) + N_CHUNKS + k + 1)
                        slot = (FIRST_SLOT + k) % RING
                        cols = slice(h * HALF, (h + 1) * HALF)
                        last = split_product(score_ps[v % 2][:, 0:HALF], ring(slot, slice(c * P, (c + 1) * P)),
                                             (act_hi[:, k, cols], act_lo[:, k, cols]), k == 0, k == KC - 1)
                    last.then_inc(scored, 1)
                for w in range(2 * TILES):
                    t, j = w // 2, w % 2
                    pe.wait_ge(unit_free[w % 2], i * TILES + (N_UNITS + w) // 2)
                    pe.wait_ge(u_ready, i * 8 + 4 * (t // 3 + 1))
                    for k in range(4):
                        if t == 0:
                            pe.wait_ge(lo_cut, i * (2 * KC) + N_CHUNKS + KC + 4 * j + k + 1)
                        slot = (FIRST_SLOT + KC + 4 * j + k) % RING
                        cols = slice(t * P, (t + 1) * P)
                        last = split_product(unit_ps[w % 2][:, :], (u_hi[:, k, cols], u_lo[:, k, cols]), ring(slot),
                                             k == 0, k == 3)
                    last.then_inc(unit_done, 1)

        @block.scalar
        def _(act):
            act.wait_ge(dve_step, 1)
            class_at = [u for u, (branch, _, _) in enumerate(units) if branch in "12"]
            class_units = [units[u][:2] for u in class_at]
            band_end = max(u for u, unit in enumerate(units) if unit[0] == "0") + 1

            act.activation(rms[:, 0:1], eps[:, :], ACT.Sqrt)

            def cut_hi(slot):
                act.activation(ring_hi[:, slot, :], ring_whole[:, slot, :], ACT.Copy).then_inc(hi_cut, 1)

            def cut_mlp(i, c):
                slot = (N_CHUNKS + c) % RING
                act.wait_ge(landed[slot], i * 16 + (plan.landed_total[slot] + 16))
                cut_hi(slot)

            def norm(x_ap, junk, n):
                act.activation(junk, x_ap, ACT.Square, accum_out=ssq[:, n % 2:n % 2 + 1]).then_inc(squares, 1)
                act.wait_ge(squares, n + 1)
                act.activation(rms[:, n % 2:n % 2 + 1], ssq[:, n % 2:n % 2 + 1], ACT.Sqrt, scale=1.0 / D,
                               bias=eps[:, :]).then_inc(roots, 1)

            def take_unit(name, i):
                n = plan.unit_no[("unit", name, i)]
                bank = unit_ps[n % 2]
                if name in ("qa", "kva", "qk0", "qk1", "qk2"):
                    q = plan.qk_no[("turn_qk", name, i)]
                    act.wait_ge(unit_done, n + 1)
                    if q >= 2:
                        before = next(x for x, m in plan.qk_no.items() if m == q - 2)
                        act.wait_ge(turned, plan.turn_no[before] + 1)
                    if name == "qa":
                        act.activation(tok[:, q % 2, :].rearrange("p (g k d) -> p g k d", g=A_GROUP, k=A_KV),
                                       bank[:, :].rearrange("p (k g d) -> p g k d", k=A_KV, g=A_GROUP),
                                       ACT.Copy).then_inc(unit_free[n % 2], 1)
                    elif name == "kva":
                        act.activation(v_a[:, i, :], bank[:, P:2 * P], ACT.Copy)
                        act.activation(v_b[:, i, 0:GW], bank[:, 2 * P:], ACT.Copy)
                        act.activation(tok[:, q % 2, 0:P], bank[:, 0:P], ACT.Copy).then_inc(unit_free[n % 2], 1)
                    else:
                        act.activation(tok[:, q % 2, :], bank[:, :], ACT.Copy).then_inc(unit_free[n % 2], 1)
                    if name in ("qa", "kva"):
                        nh = A_HEADS if name == "qa" else A_KV
                        act.wait_ge(qk_squares, q + 1)
                        act.activation(qk_rms[:, 0:nh], qk_ssq[:, 0:nh], ACT.Sqrt, scale=1.0 / HD,
                                       bias=eps[:, :]).then_inc(qk_roots, 1)
                elif name == "v12":
                    act.wait_ge(unit_done, n + 1)
                    act.activation(v_b[:, i, GW:], bank[:, :], ACT.Copy).then_inc(unit_free[n % 2], 1)
                elif name[0] == "g":
                    order = ["ga0", "gb0", "gb1", "ga1"].index(name)
                    if order == 0:
                        act.wait_ge(scored, band_end)
                    else:
                        act.wait_ge(*free_of(unit_free, plan.unit_no[("unit", ["ya0", "yb0", "yb1"][order - 1], i)]))
                    act.wait_ge(unit_done, n + 1)
                    act.activation(gate[:, i // 2, i % 2 * HALF:(i % 2 + 1) * HALF], bank[:, 0:HALF], ACT.Exp,
                                   scale=-1.0).then_inc(unit_free[n % 2], 1)

            for s in steps:
                kind = s[0]
                if kind == "hi":
                    n = s[1]
                    act.wait_ge(landed[n % RING], plan.landed[n])
                    cut_hi(n % RING)
                elif kind == "norm":
                    t = s[1]
                    act.wait_ge(x_landed[t], 16)
                    if t >= 2:
                        act.wait_ge(turned, plan.turn_no[("turn", t - 2, 1)] + 1)
                    norm(x_in[:, t, :], xn[:, t % 2, :], t)
                elif kind == "norm2":
                    t = s[1]
                    act.wait_ge(*free_of(unit_free, plan.unit_no[("unit", "wo1", t)]))
                    if t >= 2:
                        act.wait_ge(turned, plan.turn_no[("turn2", t - 2, 1)] + 1)
                    norm(x2[:, t, :], xn2[:, t % 2, :], TILES + t)
                elif kind in ("turn", "turn2"):
                    n, t, half = plan.turn_no[s], s[1], s[2]
                    act.wait_ge(turned, n + 1)
                    act.activation(act_hi[:, 4 * half:4 * half + 4, t * P:(t + 1) * P],
                                   turn_ps[n % 2][:, :].rearrange("p (c t) -> p c t", c=4),
                                   ACT.Copy).then_inc(turn_hi, 1)
                elif kind == "turn_qk":
                    n, name, t = plan.turn_no[s], s[1], s[2]
                    act.wait_ge(turned, n + 1)
                    if name in ("qk1", "qk2"):
                        order = class_units.index((name[2], t))
                        if order >= 2:
                            act.wait_ge(scored, class_at[order - 2] + 1)
                        dst = qkT_c[:, t % 2, :]
                    elif name == "qa":
                        dst = qT_a[:, :, t * P:(t + 1) * P]
                    elif name == "kva":
                        act.activation(kT_a[0:HD, 0, t * P:(t + 1) * P], turn_ps[n % 2][0:HD, 0:P], ACT.Copy)
                        act.activation(kT_a[HD:P, 1, t * P:(t + 1) * P], turn_ps[n % 2][HD:P, 0:P],
                                       ACT.Copy).then_inc(turn_free[n % 2], 1)
                        continue
                    else:
                        dst = qkT_0[:, :, t * P:(t + 1) * P]
                    src = turn_ps[n % 2][:, :]
                    if name in ("qa", "qk0"):
                        src = src.rearrange("p (c t) -> p c t", c=4)
                    act.activation(dst, src, ACT.Copy).then_inc(turn_free[n % 2], 1)
                elif kind == "unit":
                    take_unit(s[1], s[2])
                elif kind == "scores":
                    u = s[1]
                    branch, t, segs = units[u]
                    act.wait_ge(maxed, u + 1)
                    if branch == "A" and u >= 2:
                        act.wait_ge(turned, plan.turn_no[("turn_p", u - 2)] + 1)
                    src = score_ps[u % 2] if branch == "A" else probs[:, u % 2, :]
                    at = 0
                    for j, (h, k0, nk) in enumerate(segs):
                        col = stat_col(branch, t, h)
                        last = act.activation(probs[:, u % 2, at:at + nk * P], src[:, at:at + nk * P], ACT.Exp,
                                              bias=neg_max[:, col:col + 1], scale=SCALE if branch == "A" else 1.0,
                                              accum_out=den[:, col:col + 1])
                        at += nk * P
                    last.then_inc(expd, 1)
                elif kind == "turn_p":
                    u, n = s[1], plan.turn_no[s]
                    width = P * sum(seg[2] for seg in units[u][2])
                    act.wait_ge(turned, n + 1)
                    if u >= 2:
                        act.wait_ge(out_done, u - 1)
                    act.activation(probsT[:, u % 2, 0:width], turn_ps[n % 2][:, 0:width],
                                   ACT.Copy).then_inc(turn_free[n % 2], 1)
                elif kind == "turn_a":
                    n, t = plan.turn_no[s], s[1]
                    act.wait_ge(turned, n + 1)
                    act.activation(oTa_hi[:, :, t * P:(t + 1) * P],
                                   turn_ps[n % 2][:, :].rearrange("p (c t) -> p c t", c=4),
                                   ACT.Copy).then_inc(turn_hi, 1)
                elif kind == "turn_b":
                    n, seq, c = plan.turn_no[s], s[1], s[2]
                    first, width = (0, PROMPT) if seq == 0 else (PROMPT, SAMPLE)
                    act.wait_ge(turned, n + 1)
                    act.activation(oTb_hi[:, c, first:first + width], turn_ps[n % 2][:, 0:width],
                                   ACT.Copy).then_inc(turn_hi, 1)
                elif kind == "send_stats":
                    act.wait_ge(stats_packed, 4)
                    act.dma_start(stats_dram[0:PROMPT, :].rearrange("(a r) c -> a r c", r=4),
                                  stats_c[:, 0:4, :]).then_inc(stats_out, 16)
                    act.dma_start(stats_dram[PROMPT:, :].rearrange("(a r) c -> a r c", r=2),
                                  stats_c[:, 4:6, :]).then_inc(stats_out, 16)
                elif kind == "fetch_stats":
                    act.wait_ge(stats_out, 32)
                    act.dma_start(stats_n, stats_dram.rearrange("(t p) c -> p t c", p=P)).then_inc(stats_back, 16)
                elif kind == "combine":
                    act.wait_ge(diffs, 3)
                    act.activation(e_g, e_g, ACT.Exp).then_inc(exps_g, 1)
                    act.wait_ge(shares, 3)
                    act.dma_start(weights_dram.rearrange("(t p) c -> p t c", p=P), w_n).then_inc(shares_out, 16)
                elif kind == "fetch_shares":
                    act.wait_ge(shares_out, 16)
                    act.dma_start(w_c[:, 0:4, :],
                                  weights_dram[0:PROMPT, :].rearrange("(a r) c -> a r c", r=4)).then_inc(shares_back, 16)
                    act.dma_start(w_c[:, 4:6, :],
                                  weights_dram[PROMPT:, :].rearrange("(a r) c -> a r c", r=2)).then_inc(shares_back, 16)
                elif kind == "split_mix":
                    c = s[1]
                    act.wait_ge(mixed_done, 2 * c + 2 if c >= 4 else 8)
                    act.wait_ge(unit_done, block_end(plan.index["ga1"]))
                    act.activation(act_hi[:, c, :], mixed[c // 4][:, c % 4, :], ACT.Copy).then_inc(mix_hi, 1)
                elif kind == "hi_up":
                    cut_mlp(0, s[1])
                elif kind == "load_x":
                    act.wait_ge(mixed_done, 16)
                    for t in range(TILES):
                        act.dma_start(x2[:, t, :], x_rows(t)).then_inc(x2_landed[t], 16)
                    act.dma_start(gain_mlp[:, :], g_mlp[0].partition_broadcast(P)).then_inc(mlp_gains_in, 16)
                    act.dma_start(gain_fin[:, :], g_final.partition_broadcast(P)).then_inc(mlp_gains_in, 16)

            def relus(i):
                for v in range(8):
                    act.wait_ge(scored, i * 8 + (len(units) + v + 1))
                    act.activation(relu[:, v % 2, :], score_ps[v % 2][:, 0:HALF], ACT.Relu).then_inc(relu_done, 1)
                    cut_mlp(i, KC + v)

            with act.Fori(0, MLP_STEPS - 1) as i:
                relus(i)
                for c in range(KC):
                    cut_mlp(i + 1, c)
            relus(MLP_STEPS - 1)

            for t in range(TILES):
                n = 2 * TILES + t
                act.wait_ge(*free_of(unit_free, N_UNITS + 2 * TILES * (MLP_STEPS - 1) + 2 * t + 1))
                if t >= 2:
                    act.wait_ge(y_ready, t - 1)
                norm(x2[:, t, :], xn2[:, t % 2, :], n)

        @block.vector
        def _(dve):
            chain = [0]

            def link(ins):
                chain[0] += 1
                ins.then_inc(dve_step, 1)
                dve.wait_ge(dve_step, chain[0])

            link(dve.memset(eps[:, :], EPS))

            def normed(n, dst, src, gain):
                dve.wait_ge(roots, n + 1)
                link(dve.reciprocal(rms[:, n % 2:n % 2 + 1], rms[:, n % 2:n % 2 + 1]))
                return dve.scalar_tensor_tensor(dst, src, rms[:, n % 2:n % 2 + 1], gain, ALU.mult, ALU.mult)

            def lo_of_turn(n, hi, lo, src):
                return dve.tensor_tensor(lo, src, hi.bitcast(F32), ALU.subtract)

            def rotate_a(name, t):
                q = plan.qk_no[("turn_qk", name, t)]
                n = plan.unit_no[("unit", name, t)]
                nh = A_HEADS if name == "qa" else A_KV
                width = nh * HD
                buf = tok[:, q % 2, 0:width]
                pos = t % PROMPT_TILES
                cos, sin = (rope_qc, rope_qs) if name == "qa" else (rope_kc, rope_ks)
                dve.wait_ge(*free_of(unit_free, n))
                if q:
                    dve.wait_ge(tok_ready, q)
                link(dve.tensor_tensor(rot[:, 0:width], buf, buf, ALU.mult))
                dve.tensor_reduce(qk_ssq[:, 0:nh], rot[:, 0:width].rearrange("p (h d) -> p h d", d=HD), AX_X,
                                  ALU.add).then_inc(qk_squares, 1)
                dve.wait_ge(qk_roots, q + 1)
                link(dve.reciprocal(qk_rms[:, 0:nh], qk_rms[:, 0:nh]))
                heads = buf.rearrange("p (h d) -> p h d", d=HD)
                link(dve.tensor_tensor(heads, heads, qk_rms[:, 0:nh].unsqueeze(2).broadcast_to([P, nh, HD]), ALU.mult))
                pairs = buf.rearrange("p (h a x e) -> p h a x e", h=nh, a=2, x=2)
                turned_pairs = rot[:, 0:width].rearrange("p (h a x e) -> p h a x e", h=nh, a=2, x=2)
                sines = sin[:, pos, :].rearrange("p (a x e) -> p a x e", a=2, x=2)
                for x in range(2):
                    last = dve.tensor_tensor(turned_pairs[:, :, :, x, :], pairs[:, :, :, 1 - x, :],
                                             sines[:, :, x, :].unsqueeze(1).broadcast_to([P, nh, 2, 16]), ALU.mult)
                link(last)
                link(dve.tensor_tensor(heads, heads, cos[:, pos, :].unsqueeze(1).broadcast_to([P, nh, HD]), ALU.mult))
                dve.tensor_tensor(buf, buf, rot[:, 0:width], ALU.add).then_inc(tok_ready, 1)

            def rotate_b(name, t):
                q = plan.qk_no[("turn_qk", name, t)]
                n = plan.unit_no[("unit", name, t)]
                row = t % PROMPT_TILES if name == "qk0" else 4 + t
                front = tok[:, q % 2, :].rearrange("p (h d) -> p h d", d=HD)[:, :, 0:16]
                other = rot[:, 0:P].rearrange("p (h d) -> p h d", d=16)
                cos = rope_b[:, row, 0, :].unsqueeze(1).broadcast_to([P, 8, 16])
                dve.wait_ge(*free_of(unit_free, n))
                dve.wait_ge(tok_ready, q)
                for x in range(2):
                    last = dve.tensor_tensor(other[:, :, 8 * x:8 * x + 8], front[:, :, 8 - 8 * x:16 - 8 * x],
                                             rope_b[:, row, 1, 8 * x:8 * x + 8].unsqueeze(1)
                                             .broadcast_to([P, 8, 8]), ALU.mult)
                link(last)
                link(dve.tensor_tensor(front, front, cos, ALU.mult))
                dve.tensor_tensor(front, front, other, ALU.add).then_inc(tok_ready, 1)

            def maxima(u):
                branch, t, segs = units[u]
                dve.wait_ge(scored, u + 1)
                ns, width = len(segs), segs[0][2] * P
                col = stat_col(branch, t, segs[0][0])
                cols = neg_max[:, col:col + ns]
                bank = score_ps[u % 2][:, 0:ns * width]
                if branch == "A":
                    link(dve.tensor_reduce(cols, bank.rearrange("p (s w) -> p s w", s=ns), AX_X, ALU.max))
                    dve.tensor_scalar(cols, cols, -SCALE, None, ALU.mult).then_inc(maxed, 1)
                    return
                if u >= 2:
                    dve.wait_ge(turned, plan.turn_no[("turn_p", u - 2)] + 1)
                dst = probs[:, u % 2, 0:ns * width]
                if branch == "0":
                    first = (segs[0][1] - t + 1) * P
                    shape = [P, ns, width]
                    mask = band_mask[:, first:first + width]
                    mask = mask.unsqueeze(1).broadcast_to(shape)
                    view = "p (s w) -> p s w"
                    split = dict(s=ns)
                elif branch == "1" and t < PROMPT_TILES:
                    mask = band_mask[:, P:2 * P].unsqueeze(1).broadcast_to([P, ns, width])
                    view, split = "p (s w) -> p s w", dict(s=ns)
                else:
                    m = {("1", False): 0, ("2", True): 1, ("2", False): 2}[(branch, t < PROMPT_TILES)]
                    mask = class_mask[:, m, :].unsqueeze(1).broadcast_to([P, ns * width // 8, 8])
                    view, split = "p (s w) -> p s w", dict(w=8)
                link(dve.scalar_tensor_tensor(dst.rearrange(view, **split), bank.rearrange(view, **split), SCALE,
                                              mask, ALU.mult, ALU.add))
                link(dve.tensor_reduce(cols, dst.rearrange("p (s w) -> p s w", s=ns), AX_X, ALU.max))
                dve.tensor_scalar(cols, cols, -1.0, None, ALU.mult).then_inc(maxed, 1)

            def take_out(u):
                branch, t, segs = units[u]
                ns, h = len(segs), segs[0][0]
                col = stat_col(branch, t, h)
                src = out_ps[u % 2][:, 0:ns * P].rearrange("p (s w d) -> p s w d", w=2, d=HD)
                dve.wait_ge(out_done, u + 1)
                if branch == "A":
                    link(dve.reciprocal(den[:, col:col + ns], den[:, col:col + ns]))
                    dve.tensor_tensor(o_a[:, t, h * HD:(h + ns) * HD].rearrange("p (s d) -> p s d", d=HD),
                                      src[:, :, h // A_GROUP, :],
                                      den[:, col:col + ns].unsqueeze(2).broadcast_to([P, ns, HD]),
                                      ALU.mult).then_inc(out_read, 1)
                else:
                    dst = o_b[:, int(branch), t, h * HD:(h + ns) * HD].rearrange("p (s d) -> p s d", d=HD)
                    for x in range(min(2, ns)):
                        last = dve.tensor_copy(dst[:, x::2, :], src[:, x::2, (h + x) % 2, :])
                    last.then_inc(out_read, 1)

            for s in steps:
                kind = s[0]
                if kind in ("norm", "norm2"):
                    t = s[1]
                    if kind == "norm":
                        dve.wait_ge(x_landed[t], 16)
                        dve.wait_ge(gain_in, 16)
                        normed(t, xn[:, t % 2, :], x_in[:, t, :], gain_bc[:, :]).then_inc(xn_ready, 1)
                    else:
                        dve.wait_ge(mlp_gains_in, 32)
                        normed(TILES + t, xn2[:, t % 2, :], x2[:, t, :], gain_mlp[:, :]).then_inc(xn_ready, 1)
                elif kind in ("turn", "turn2"):
                    n, t, half = plan.turn_no[s], s[1], s[2]
                    dve.wait_ge(turn_hi, plan.split_no[s] + 1)
                    at = (slice(None), slice(4 * half, 4 * half + 4), slice(t * P, (t + 1) * P))
                    last = lo_of_turn(n, act_hi[at], act_lo[at],
                                      turn_ps[n % 2][:, :].rearrange("p (c t) -> p c t", c=4))
                    last.then_inc(turn_free[n % 2], 1)
                elif kind == "unit":
                    name, i = s[1], s[2]
                    n = plan.unit_no[s]
                    if name in ("qa", "kva"):
                        if name == "qa" and i == 0:
                            dve.wait_ge(rope_in, 48)
                            for c, sn, j in ((rope_qc, rope_qs, 0), (rope_kc, rope_ks, 1)):
                                gain = qk_gain[:, j, :].unsqueeze(1).broadcast_to([P, PROMPT_TILES, HD])
                                dve.tensor_tensor(c[:, :, :], rope_raw[:, 0, :, :], gain, ALU.mult)
                                other = qk_gain[:, j, :].rearrange("p (a x e) -> p a x e", a=2, x=2)
                                out = sn[:, :, :].rearrange("p t (a x e) -> p t a x e", a=2, x=2)
                                raw_s = rope_raw[:, 1, :, :].rearrange("p t (a x e) -> p t a x e", a=2, x=2)
                                for x in range(2):
                                    last = dve.tensor_tensor(
                                        out[:, :, :, x, :], raw_s[:, :, :, x, :],
                                        other[:, :, 1 - x, :].unsqueeze(1).broadcast_to([P, PROMPT_TILES, 2, 16]),
                                        ALU.mult)
                            link(last)
                        if name == "kva" and i == 0:
                            dve.wait_ge(roots, TILES)
                            dve.memset(kT_a[HD:P, 0, :], 0.0)
                            link(dve.memset(kT_a[0:HD, 1, :], 0.0))
                        rotate_a(name, i)
                    elif name in ("qk0", "qk1", "qk2"):
                        dve.wait_ge(tables_in, 48)
                        rotate_b(name, i)
                    elif name[0] == "g":
                        part = gate[:, i // 2, i % 2 * HALF:(i % 2 + 1) * HALF]
                        dve.wait_ge(*free_of(unit_free, n))
                        link(dve.tensor_scalar(part, part, 1.0, None, ALU.add))
                        dve.reciprocal(part, part).then_inc(dve_step, 1)
                        chain[0] += 1
                    elif name[0] == "y":
                        c, h = i // 2, i % 2
                        cols = slice(h * HALF, (h + 1) * HALF)
                        into = mixed[int(name[2])][:, c, cols]
                        if i == 0:
                            dve.wait_ge(dve_step, chain[0])
                        dve.wait_ge(unit_done, n + 1)
                        if name in ("ya0", "yb1"):
                            dve.tensor_tensor(into, unit_ps[n % 2][:, 0:HALF], gate[:, c, cols],
                                              ALU.mult).then_inc(unit_free[n % 2], 1)
                        else:
                            part = mix_part[:, i % 2, :]
                            dve.tensor_tensor(part, unit_ps[n % 2][:, 0:HALF], gate[:, c, cols],
                                              ALU.mult).then_inc(unit_free[n % 2], 1)
                            dve.wait_ge(*free_of(unit_free, n))
                            dve.tensor_tensor(into, into, part, ALU.add).then_inc(mixed_done, 1)
                    elif name[:2] == "wo":
                        j = int(name[2])
                        dve.wait_ge(unit_done, n + 1)
                        if j == 0:
                            dve.wait_ge(x2_landed[i], 16)
                        part = x2[:, i, j * COLS:(j + 1) * COLS]
                        dve.tensor_tensor(part, part, unit_ps[n % 2][:, :], ALU.add).then_inc(unit_free[n % 2], 1)
                elif kind == "scores":
                    maxima(s[1])
                elif kind == "pv":
                    take_out(s[1])
                elif kind == "send_stats":
                    dve.wait_ge(expd, len(units))
                    for j, (src, g) in enumerate(((neg_max, 1), (neg_max, 2), (den, 1), (den, 2))):
                        first = STAT_A + g * STAT_B
                        dve.tensor_copy(stats_c[:, :, 4 * j:4 * j + 4],
                                        src[:, first:first + STAT_B].rearrange("p (t h) -> p t h", h=4))\
                           .then_inc(stats_packed, 1)
                elif kind == "turn_a":
                    n, t = plan.turn_no[s], s[1]
                    dve.wait_ge(turn_hi, plan.split_no[s] + 1)
                    at = (slice(None), slice(0, 4), slice(t * P, (t + 1) * P))
                    lo_of_turn(n, oTa_hi[at], oTa_lo[at], turn_ps[n % 2][:, :].rearrange("p (c t) -> p c t", c=4))\
                        .then_inc(turn_free[n % 2], 1)
                elif kind == "turn_b":
                    n, seq, c = plan.turn_no[s], s[1], s[2]
                    first, width = (0, PROMPT) if seq == 0 else (PROMPT, SAMPLE)
                    dve.wait_ge(turn_hi, plan.split_no[s] + 1)
                    at = (slice(None), c, slice(first, first + width))
                    lo_of_turn(n, oTb_hi[at], oTb_lo[at], turn_ps[n % 2][:, 0:width]).then_inc(turn_free[n % 2], 1)
                elif kind == "combine":
                    dve.wait_ge(stats_back, 16)
                    own = slice(STAT_A, STAT_A + STAT_B)
                    m = [neg_max[:, own].rearrange("p (t h) -> p t h", h=4), stats_n[:, :, 0:4], stats_n[:, :, 4:8]]
                    d = [den[:, own].rearrange("p (t h) -> p t h", h=4), stats_n[:, :, 8:12], stats_n[:, :, 12:16]]
                    top, total = small[:, 0], small[:, 1]
                    link(dve.tensor_tensor(top, m[0], m[1], ALU.min))
                    link(dve.tensor_tensor(top, top, m[2], ALU.min))
                    for g in range(B_GROUPS):
                        dve.tensor_tensor(e_g[:, g], top, m[g], ALU.subtract).then_inc(diffs, 1)
                    dve.wait_ge(exps_g, 1)
                    for g in range(B_GROUPS):
                        link(dve.tensor_tensor(z_g[:, g], e_g[:, g], d[g], ALU.mult))
                    link(dve.tensor_tensor(total, z_g[:, 0], z_g[:, 1], ALU.add))
                    link(dve.tensor_tensor(total, total, z_g[:, 2], ALU.add))
                    link(dve.reciprocal(total, total))
                    for g, out in enumerate((w_0, w_n[:, :, 0:4], w_n[:, :, 4:8])):
                        dve.tensor_tensor(out, e_g[:, g], total, ALU.mult).then_inc(shares, 1)
                elif kind == "weight":
                    dve.wait_ge(shares, 1)
                    for g, share in enumerate((w_0, w_c[:, :, 0:4], w_c[:, :, 4:8])):
                        if g == 1:
                            dve.wait_ge(shares_back, 32)
                        part = o_b[:, g].rearrange("p t (h d) -> p t h d", d=HD)
                        dve.tensor_tensor(part, part, share.unsqueeze(3).broadcast_to([P, TILES, B_HEADS, HD]),
                                          ALU.mult).then_inc(weighted, 1)
                elif kind == "split_mix" and s[1] >= 4:
                    c = s[1]
                    dve.wait_ge(mix_hi, mix_order.index(c) + 1)
                    dve.tensor_tensor(act_lo[:, c, :], mixed_1[:, c - 4, :], act_hi[:, c, :].bitcast(F32),
                                      ALU.subtract).then_inc(mix_ready_1, 1)

            def square_up(i):
                for v in range(8):
                    h, c = v // 4, v % 4
                    cols = slice(h * HALF, (h + 1) * HALF)
                    dve.wait_ge(relu_done, i * 8 + v + 1)
                    dve.scalar_tensor_tensor(usq[:, v % 2, :], score_ps[v % 2][:, 0:HALF], 0.0, relu[:, v % 2, :],
                                             ALU.max, ALU.mult).then_inc(u_squared[v % 2], 1)
                    dve.wait_ge(u_squared[v % 2], i * 4 + v // 2 + 1)
                    dve.tensor_copy(u_hi[:, c, cols], usq[:, v % 2, :]).then_inc(dve_step, 1)
                    dve.wait_ge(dve_step, i * 8 + (chain[0] + v + 1))
                    dve.tensor_tensor(u_lo[:, c, cols], usq[:, v % 2, :], u_hi[:, c, cols].bitcast(F32),
                                      ALU.subtract).then_inc(u_ready, 1)

            def add_down(i, w):
                t, j = w // 2, w % 2
                dve.wait_ge(unit_done, i * (2 * TILES) + (N_UNITS + w + 1))
                part = x2[:, t, j * COLS:(j + 1) * COLS]
                dve.tensor_tensor(part, part, unit_ps[w % 2][:, :], ALU.add).then_inc(unit_free[w % 2], 1)

            with dve.Fori(0, MLP_STEPS - 1) as i:
                square_up(i)
                for w in range(2 * TILES):
                    add_down(i, w)
            square_up(MLP_STEPS - 1)
            chain[0] += 8 * MLP_STEPS

            def output(t):
                normed(2 * TILES + t, x2[:, t, :], x2[:, t, :], gain_fin[:, :]).then_inc(y_ready, 1)

            for w in range(2 * TILES):
                add_down(MLP_STEPS - 1, w)
                if w >= 3 and w % 2:
                    output(w // 2 - 1)
            output(TILES - 1)


def rope_angles(pos, dim, theta):
    freqs = np.float32(theta) ** (-(np.arange(dim // 2, dtype=np.float32) * np.float32(2.0)) / np.float32(dim))
    return pos.astype(np.float32)[:, None] * freqs[None, :].astype(np.float32)


def shape_tables():
    pos = np.arange(PROMPT)
    row, col = rope_angles(pos // 64, HD // 2, 10000.0), rope_angles(pos % 64, HD // 2, 10000.0)
    cos = np.concatenate([np.cos(row), np.cos(row), np.cos(col), np.cos(col)], 1)
    sin = np.concatenate([-np.sin(row), np.sin(row), -np.sin(col), np.sin(col)], 1)
    a = np.stack([cos, sin]).reshape(2, PROMPT_TILES, P, HD).transpose(2, 0, 1, 3)
    rows = np.arange(P)
    order = [t * P + rows for t in range(4)] + [4 * rows + r for r in range(4)] + [2 * rows + r for r in range(2)]
    b = []
    for p in order:
        ang = rope_angles(p, 16, 500000.0)
        b.append(np.stack([np.concatenate([np.cos(ang), np.cos(ang)], 1),
                           np.concatenate([-np.sin(ang), np.sin(ang)], 1)], 1))
    b = np.stack(b, 1)
    keys = np.arange(3 * P) - P
    band = np.where(np.abs(keys[None, :] - rows[:, None]) <= 64, 0.0, NEG)
    same = [np.where(rows[:, None] % m == np.arange(8)[None, :] % m, 0.0, NEG) for m in (2, 4, 8)]
    mask = np.concatenate([band] + same, 1)
    out = {"rope_a_tab": a, "rope_b_tab": b, "mask_tab": mask, "ident_tab": np.eye(P)}
    return {k: np.ascontiguousarray(v, dtype=np.float32) for k, v in out.items()}


_INS = ["x_prompt", "x_sample", "w_in", "w_a_out", "w_b_out", "w_out", "g_mix", "q_gain", "k_gain", "g_mlp",
        "w_up", "w_down", "g_final"]
_TABLES = ["rope_a_tab", "rope_b_tab", "mask_tab", "ident_tab"]


def kernel(**inputs):
    import concourse.bacc as bacc
    from concourse.bass_utils import run_bass_kernel_spmd

    nc = bacc.Bacc("TRN2", target_bir_lowering=False, num_devices=1)
    arrays, args = {}, []
    tables = shape_tables()
    for name in _INS + _TABLES:
        a = np.ascontiguousarray(inputs[name] if name in inputs else tables[name])
        arrays[f"in_{name}"] = a
        args.append(nc.dram_tensor(f"in_{name}", a.shape, mybir.dt.from_np(a.dtype), kind="ExternalInput").ap())
    for name, n in (("y_prompt", PROMPT), ("y_sample", SAMPLE)):
        args.append(nc.dram_tensor(name, (1, n, D), F32, kind="ExternalOutput").ap())
    build(nc, *args)
    r = run_bass_kernel_spmd(nc, [arrays], core_ids=[0])
    return r.results[0]["y_prompt"], r.results[0]["y_sample"]
```

```python
from contextlib import ExitStack

import numpy as np

import concourse.bass as bass
from concourse import mybir

F32 = mybir.dt.float32
F32R = mybir.dt.float32r
ALU = mybir.AluOpType
ACT = mybir.ActivationFunctionType
AX_X = mybir.AxisListType.X

P = 128
D = 1024
KC = D // P
TILES, PROMPT_TILES = 6, 4
TOK = TILES * P
PROMPT, SAMPLE = 512, 256
HALF = TOK // 2
HD = 64
A_HEADS, A_KV, A_GROUP = 8, 2, 4
B_HEADS, B_GROUPS = 4, 3
FF = 4096
COLS = 512
EPS = 1e-6
SCALE = HD ** -0.5
RING = 16
MLP_STEPS = FF // COLS
NEG = -1.0e30

Q_A, K_A, V_A, Q_B, K_B, V_B, G_A, G_B = 0, 512, 640, 768, 1536, 2304, 3072, 4096
GW = B_HEADS * HD

STAT_A = TILES * A_HEADS
STAT_B = TILES * B_HEADS
STATS = STAT_A + B_GROUPS * STAT_B


def weight_blocks():
    def full(name, matrix, col, rows):
        return (name, [[(matrix, k * P, col, COLS)] for k in range(rows // P)])

    def paired(name, cols):
        return (name, [[("w_in", k * P, c, COLS // len(cols)) for c in cols] for k in range(KC)])

    blocks = [full("qa", "w_in", Q_A, D), paired("kva", [K_A, V_B]), paired("qk0", [Q_B, K_B]),
              full("v12", "w_in", V_B + GW, D), paired("qk1", [Q_B + GW, K_B + GW]),
              paired("qk2", [Q_B + 2 * GW, K_B + 2 * GW])]
    gate_a = [full(f"ga{j}", "w_in", G_A + j * COLS, D) for j in range(2)]
    gate_b = [full(f"gb{j}", "w_in", G_B + j * COLS, D) for j in range(2)]
    out_a = [full(f"ya{j}", "w_a_out", j * COLS, A_HEADS * HD) for j in range(2)]
    out_b = [full(f"yb{j}", "w_b_out", j * COLS, B_HEADS * HD) for j in range(2)]
    blocks += [gate_a[0], out_a[0], gate_b[0], out_b[0], gate_b[1], out_b[1], gate_a[1], out_a[1]]
    blocks += [full(f"wo{j}", "w_out", j * COLS, D) for j in range(2)]
    return blocks


def attention_units():
    branch_a, band, classes = [], [], []
    for t in range(PROMPT_TILES):
        branch_a += [("A", t, [(h, 0, 4)]) for h in range(A_HEADS)]
    for t in range(PROMPT_TILES, TILES):
        branch_a += [("A", t, [(h, 4, 2), (h + 1, 4, 2)]) for h in range(0, A_HEADS, 2)]
    for t in range(PROMPT_TILES):
        lo, hi = max(0, t - 1), min(PROMPT_TILES - 1, t + 1)
        band += [("0", t, [(h, lo, hi - lo + 1)]) for h in range(B_HEADS)]
    for t in range(PROMPT_TILES, TILES):
        band += [("0", t, [(h, 4, 2), (h + 1, 4, 2)]) for h in range(0, B_HEADS, 2)]
    for g in "12":
        classes += [(g, t, [(h, t, 1) for h in range(B_HEADS)]) for t in range(TILES)]
    return branch_a, band, classes


def make_schedule():
    blocks = weight_blocks()
    sizes = {name: len(chunks) for name, chunks in blocks}
    owner = [name for name, chunks in blocks for _ in chunks]
    branch_a, band, classes = attention_units()
    steps, units, finished, turned, fresh = [], [], set(), set(), []
    state = {"cut": 0, "tick": 0}

    def cuts(limit):
        for _ in range(limit):
            n = state["cut"]
            if n < len(owner) and (n < RING or owner[n - RING] in finished):
                steps.append(("hi", n))
                state["cut"] += 1

    def unit(name, i, count, rate=0, cut=2, between=None):
        need = len(owner) - owner[::-1].index(name)
        cuts(max(0, need - state["cut"]))
        assert state["cut"] >= need
        for j in range(rate - 1):
            steps.append(("part", name, i, sizes[name] * j // rate, sizes[name] * (j + 1) // rate))
            (between or attend)()
        steps.append(("unit", name, i))
        cuts(cut)
        if i == count - 1:
            finished.add(name)

    def next_unit():
        if branch_a:
            last_keys = branch_a[0][2][0][1] + branch_a[0][2][0][2] - 1
            return branch_a.pop(0) if ("kva", last_keys) in turned else None
        if classes and ("qk" + classes[0][0], classes[0][1]) in turned:
            return classes.pop(0)
        if band and ("qk0", TILES - 1) in turned:
            return band.pop(0)
        return None

    def prepare():
        while branch_a and len(units) < state["tick"] + 2:
            new = next_unit()
            if new is None:
                return
            units.append(new)
            steps.append(("q_split", len(units) - 1))

    def attend(count=1):
        for _ in range(count):
            for entry in list(fresh):
                entry[1] += 1
                if entry[1] > 2:
                    turned.add(entry[0])
                    fresh.remove(entry)
            prepare()
            if len(units) == state["tick"] and (branch_a or band or classes):
                new = next_unit()
                if new is None:
                    return
                units.append(new)
            i = state["tick"]
            early = i < len(units) and units[i][0] != "A" and units[i - 2][0] != "A"
            if early:
                steps.append(("scores_first", i))
            if 0 <= i - 2 < len(units):
                steps.append(("turn_p", i - 2))
            if i < len(units):
                steps.append(("scores", i))
            if 0 <= i - 3 < len(units):
                steps.append(("pv", i - 3))
            state["tick"] += 1

    waiting = []

    def turn_next():
        b, t = waiting.pop(0)
        steps.append(("turn_qk", b, t))
        fresh.append([(b, t), 0])

    def rotated_unit(name, t, rate=0):
        unit(name, t, TILES, rate)
        waiting.append((name, t))
        while len(waiting) > 2:
            turn_next()

    steps.append(("norm", 0))
    cuts(2)
    steps += [("turn", 0, 0), ("turn", 0, 1), ("norm", 1)]
    cuts(3)
    steps += [("part", "qa", 0, 0, 3), ("turn", 1, 0), ("turn", 1, 1)]
    cuts(1)
    steps += [("part", "qa", 0, 3, 4), ("part", "qa", 1, 0, 4), ("tables",), ("norm", 2)]
    for k in range(4, KC - 1):
        cuts(1)
        steps += [("part", "qa", t, k, k + 1) for t in range(2)]
        if k == 5:
            steps.append(("norm", 3))
    steps += [("turn", 2, 0), ("turn", 2, 1), ("norm", 4), ("turn", 3, 0), ("turn", 3, 1)]
    rotated_unit("qa", 0)
    rotated_unit("qa", 1)
    steps += [("part", "qa", 2, 0, 4), ("turn", 4, 0), ("turn", 4, 1), ("norm", 5)]
    rotated_unit("qa", 2)
    steps += [("part", "qa", 3, 0, 4), ("turn", 5, 0), ("turn", 5, 1)]
    for t in range(3, TILES):
        rotated_unit("qa", t)
    for name, rate in (("kva", 3), ("qk0", 3), ("v12", 3), ("qk1", 3), ("qk2", 3)):
        for t in range(TILES):
            if name == "v12":
                unit(name, t, TILES, rate)
                if waiting:
                    turn_next()
            else:
                rotated_unit(name, t, rate)
            attend(1)
    while band:
        attend(1)
    left = iter(range(TILES))

    def attend_or_turn():
        if classes or state["tick"] < len(units) + 3:
            attend(1)
            return
        if ("send_stats",) not in steps:
            steps.append(("send_stats",))
        t = next(left, None)
        if t is not None:
            steps.append(("turn_a", t))

    for i in range(8):
        if waiting:
            turn_next()
        unit("ga0", i, 8, 2, between=attend_or_turn)
        if i < 7:
            attend_or_turn()
        else:
            steps.append(("fetch_stats",))
    assert not list(left)
    behind = {("ya0", 5): [("combine",)], ("gb0", 0): [("fetch_shares",)],
              ("gb0", 1): [("weight",)], ("gb0", 3): [("turn_b", 0, 0)], ("gb0", 4): [("turn_b", 1, 0)],
              ("gb0", 5): [("turn_b", 0, 1)], ("gb0", 6): [("turn_b", 1, 1)]}
    for i, cs in {0: ["h0"], 1: ["h1"], 2: ["h4", "h2", "l0", "l1", "l2"], 3: ["h3", "l4", "l3"], 4: ["h5"],
                  5: ["l5"], 6: ["h6"], 7: ["l6", "h7", "l7"]}.items():
        behind["ya1", i] = [({"h": "mix_hi", "l": "mix_lo"}[c[0]], int(c[1])) for c in cs]
    for name in ("ya0", "gb0", "yb0", "gb1", "yb1", "ga1", "ya1"):
        for i in range(8):
            unit(name, i, 8, cut=2 if name != "ya1" else int(i > 1))
            steps.extend(behind.get((name, i), []))
    steps.append(("load_x",))
    for i in range(TILES):
        unit("wo0", i, TILES)
    for i in range(TILES):
        unit("wo1", i, TILES)
        if i < 5:
            steps.append(("norm2", i))
        if i < 4:
            steps += [("hi_up", 2 * i), ("hi_up", 2 * i + 1)]
        if 2 <= i < 5:
            steps += [("turn2", i - 2, 0), ("turn2", i - 2, 1)]
    for v in range(8):
        steps.append(("up", v))
        if v < 3:
            steps += [("turn2", 3 + v, 0), ("turn2", 3 + v, 1)]
        if v == 0:
            steps.append(("norm2", 5))
    assert state["cut"] == len(owner) and not (branch_a or band or classes)
    return blocks, units, steps


class Plan:

    def __init__(self):
        self.blocks, self.units, self.steps = make_schedule()
        self.chunks = [c for _, chunks in self.blocks for c in chunks]
        self.start, self.index, self.size = {}, {}, {}
        n = 0
        for b, (name, chunks) in enumerate(self.blocks):
            self.start[name], self.index[name], self.size[name] = n, b, len(chunks)
            n += len(chunks)
        self.owner = [b for b, (_, chunks) in enumerate(self.blocks) for _ in chunks]
        self.unit_no, self.turn_no, self.qk_no = {}, {}, {}
        self.split_no = {}
        for s in self.steps:
            if s[0] == "unit":
                self.unit_no[s] = len(self.unit_no)
            elif s[0] in ("turn", "turn_qk", "turn_p", "turn_a", "turn_b", "turn2"):
                self.turn_no[s] = len(self.turn_no)
                if s[0] == "turn_qk":
                    self.qk_no[s] = len(self.qk_no)
                elif s[0] != "turn_p":
                    self.split_no[s] = len(self.split_no)
        self.landed, self.landed_total = [], [0] * RING
        for n, c in enumerate(self.chunks):
            self.landed_total[n % RING] += 16 * len(c)
            self.landed.append(self.landed_total[n % RING])


def stat_col(branch, t, h):
    return t * A_HEADS + h if branch == "A" else STAT_A + int(branch) * STAT_B + t * B_HEADS + h


def build(nc, x_prompt, x_sample, w_in, w_a_out, w_b_out, w_out, g_mix, q_gain, k_gain, g_mlp, w_up,
          w_down, g_final, rope_a_tab, rope_b_tab, mask_tab, ident_tab, y_prompt, y_sample):
    plan = Plan()
    blocks, units, steps = plan.blocks, plan.units, plan.steps
    matrices = {"w_in": w_in[0], "w_a_out": w_a_out[0], "w_b_out": w_b_out[0], "w_out": w_out[0]}
    w_up, w_down = w_up[0], w_down[0]

    def x_rows(t):
        return x_prompt[0, t * P:(t + 1) * P, :] if t < PROMPT_TILES \
            else x_sample[0, (t - PROMPT_TILES) * P:(t - PROMPT_TILES + 1) * P, :]

    def y_rows(t):
        return y_prompt[0, t * P:(t + 1) * P, :] if t < PROMPT_TILES \
            else y_sample[0, (t - PROMPT_TILES) * P:(t - PROMPT_TILES + 1) * P, :]

    with ExitStack() as ctx:
        def sb(stack, name, shape, dt=F32):
            return stack.enter_context(nc.sbuf_tensor(name, shape, dt))

        def sem(name):
            return ctx.enter_context(nc.semaphore(name))

        st = ExitStack()
        ring_whole = sb(st, "ring_whole", [P, RING, COLS])
        st.close()
        ring_lo = sb(ctx, "ring_lo", [P, RING, COLS], F32R)
        ring_hi = sb(ctx, "ring_hi", [P, RING, COLS], F32R)
        act_hi = sb(ctx, "act_hi", [P, KC, TOK], F32R)
        act_lo = sb(ctx, "act_lo", [P, KC, TOK], F32R)
        ident = sb(ctx, "ident", [P, P])
        band_mask = sb(ctx, "band_mask", [P, 3 * P])
        class_mask = sb(ctx, "class_mask", [P, 3, 8])
        rope_qc = sb(ctx, "rope_qc", [P, PROMPT_TILES, HD])
        rope_qs = sb(ctx, "rope_qs", [P, PROMPT_TILES, HD])
        rope_kc = sb(ctx, "rope_kc", [P, PROMPT_TILES, HD])
        rope_ks = sb(ctx, "rope_ks", [P, PROMPT_TILES, HD])
        rope_b = sb(ctx, "rope_b", [P, 10, 2, 16])
        neg_max = sb(ctx, "neg_max", [P, STATS])
        den = sb(ctx, "den", [P, STATS])
        eps = sb(ctx, "eps", [P, 1])
        ssq = sb(ctx, "ssq", [P, 2])
        rms = sb(ctx, "rms", [P, 2])
        k_ssq = sb(ctx, "k_ssq", [P, A_KV])
        k_rms = sb(ctx, "k_rms", [P, A_KV])
        q_scale = sb(ctx, "q_scale", [P, STAT_A])
        eps_q = sb(ctx, "eps_q", [P, 1])
        qk_sq = sb(ctx, "qk_sq", [P, 512])
        q_hi = sb(ctx, "q_hi", [P, 2, 2, P], F32R)
        q_lo = sb(ctx, "q_lo", [P, 2, 2, P], F32R)

        st = ExitStack()
        x_in = sb(st, "x_in", [P, TILES, D])
        gain_bc = sb(st, "gain_bc", [P, D])
        xn = sb(st, "xn", [P, 2, D])
        st.close()

        st = ExitStack()
        qT_a = sb(st, "qT_a", [P, 4, TOK])
        kT_a = sb(st, "kT_a", [P, A_KV, TOK], F32R)
        v_a = sb(st, "v_a", [P, TILES, A_KV * HD])
        o_a = sb(st, "o_a", [P, TILES, A_HEADS * HD])
        probs = sb(st, "probs", [P, 2, 512])
        probsT = sb(st, "probsT", [P, 2, 512])
        tok = sb(st, "tok", [P, 2, 512])
        rot = sb(st, "rot", [P, 512])
        qkT_c = sb(st, "qkT_c", [P, 2, 512])
        v_b = sb(st, "v_b", [P, TILES, B_GROUPS * GW])
        qkT_0 = sb(st, "qkT_0", [P, 4, TOK])
        st.close()
        st = ExitStack()
        sb(st, "hold_r", [P, 52224 // 4])
        rope_raw = sb(st, "rope_raw", [P, 2, PROMPT_TILES, HD])
        qk_gain = sb(st, "qk_gain", [P, 2, HD])
        st.close()

        st = ExitStack()
        o_b = sb(st, "o_b", [P, B_GROUPS, TILES, GW])
        st.close()
        st = ExitStack()
        sb(st, "hold_o", [P, (21504 + 12288) // 4])
        oTa_hi = sb(st, "oTa_hi", [P, 4, TOK], F32R)
        oTa_lo = sb(st, "oTa_lo", [P, 4, TOK], F32R)
        oTb_hi = sb(st, "oTb_hi", [P, 2, TOK], F32R)
        oTb_lo = sb(st, "oTb_lo", [P, 2, TOK], F32R)
        gate = sb(st, "gate", [P, 4, TOK])
        st.close()
        st = ExitStack()
        mixed_1 = sb(st, "mixed_1", [P, 4, TOK])
        mix_part = sb(st, "mix_part", [P, 2, HALF])
        sb(st, "hold_m", [P, 6144 // 4])
        mixed_0 = sb(st, "mixed_0", [P, 4, TOK])
        st.close()
        mixed = (mixed_0, mixed_1)

        st = ExitStack()
        u_hi = sb(st, "u_hi", [P, 4, TOK], F32R)
        u_lo = sb(st, "u_lo", [P, 4, TOK], F32R)
        relu = sb(st, "relu", [P, 2, HALF])
        usq = sb(st, "usq", [P, 2, HALF])
        sb(st, "hold_x", [P, 3072 // 4])
        x2 = sb(st, "x2", [P, TILES, D])
        gain_mlp = sb(st, "gain_mlp", [P, D])
        gain_fin = sb(st, "gain_fin", [P, D])
        xn2 = sb(st, "xn2", [P, 2, D])
        st.close()

        stats_c = rope_qc[:].rearrange("p t d -> p (t d)")[:, 0:96].rearrange("p (t c) -> p t c", c=16)
        stats_n = rope_qc[:].rearrange("p t d -> p (t d)")[:, 96:192].rearrange("p (t c) -> p t c", c=16)
        w_0 = rope_qc[:].rearrange("p t d -> p (t d)")[:, 192:216].rearrange("p (t c) -> p t c", c=4)
        w_n = rope_qs[:].rearrange("p t d -> p (t d)")[:, 0:48].rearrange("p (t c) -> p t c", c=8)
        w_c = rope_qs[:].rearrange("p t d -> p (t d)")[:, 48:96].rearrange("p (t c) -> p t c", c=8)
        e_g = rope_kc[:].rearrange("p t d -> p (t d)")[:, 0:72].rearrange("p (g t c) -> p g t c", g=3, c=4)
        z_g = rope_kc[:].rearrange("p t d -> p (t d)")[:, 72:144].rearrange("p (g t c) -> p g t c", g=3, c=4)
        small = rope_ks[:].rearrange("p t d -> p (t d)")[:, 0:48].rearrange("p (g t c) -> p g t c", g=2, c=4)

        stats_dram = nc.dram_tensor("stats_scratch", [TOK, 16], F32, kind="Internal").ap()
        weights_dram = nc.dram_tensor("weights_scratch", [TOK, 8], F32, kind="Internal").ap()

        def banks(name):
            return [ctx.enter_context(nc.psum_tensor(f"{name}{i}", [P, 512], F32)) for i in range(2)]

        unit_ps, score_ps, turn_ps, out_ps = banks("unit_ps"), banks("score_ps"), banks("turn_ps"), banks("out_ps")

        landed = [sem(f"landed{i}") for i in range(RING)]
        x_landed = [sem(f"x_landed{i}") for i in range(TILES)]
        ident_in = sem("ident_in")
        tables_in = sem("tables_in")
        gain_in = sem("gain_in")
        rope_in = sem("rope_in")
        mlp_gains_in = sem("mlp_gains_in")
        hi_cut = sem("hi_cut")
        lo_cut = sem("lo_cut")
        squares = sem("squares")
        roots = sem("roots")
        xn_ready = sem("xn_ready")
        unit_done = sem("unit_done")
        unit_free = [sem(f"unit_free{i}") for i in range(2)]
        turned = sem("turned")
        turn_hi = sem("turn_hi")
        turn_free = [sem(f"turn_free{i}") for i in range(2)]
        qk_squares = sem("qk_squares")
        q_roots = sem("q_roots")
        k_roots = sem("k_roots")
        tok_ready = sem("tok_ready")
        keys_hi = sem("keys_hi")
        queries_hi = sem("queries_hi")
        queries_split = sem("queries_split")
        scored = sem("scored")
        even_heads = sem("even_heads")
        maxed = sem("maxed")
        expd = sem("expd")
        out_done = sem("out_done")
        out_read = sem("out_read")
        stats_packed = sem("stats_packed")
        stats_out = sem("stats_out")
        stats_back = sem("stats_back")
        diffs = sem("diffs")
        exps_g = sem("exps_g")
        shares = sem("shares")
        shares_out = sem("shares_out")
        shares_back = sem("shares_back")
        weighted = sem("weighted")
        mixed_done = sem("mixed_done")
        mix_hi = sem("mix_hi")
        mix_ready_0 = sem("mix_ready_0")
        mix_ready_1 = sem("mix_ready_1")
        x2_landed = [sem(f"x2_landed{i}") for i in range(TILES)]
        relu_done = sem("relu_done")
        u_squared = [sem(f"u_squared{i}") for i in range(2)]
        u_cut = sem("u_cut")
        u_ready = sem("u_ready")
        y_ready = sem("y_ready")
        y_out = sem("y_out")
        dve_step = sem("dve_step")
        N_UNITS, N_TURNS, N_CHUNKS, N_BLOCKS = len(plan.unit_no), len(plan.turn_no), len(plan.chunks), len(blocks)
        assert N_UNITS % 2 == 0 and len(units) % 2 == 0
        FIRST_SLOT = N_CHUNKS % RING
        assert RING == 2 * KC

        def free_of(sems, n):
            return sems[n % 2], n // 2 + 1

        def wait_bank(eng, sems, n):
            if n >= 2:
                eng.wait_ge(sems[n % 2], n // 2)

        def tokens_of(name, t):
            if name in ("v12", "qk1", "qk2"):
                return slice(t, PROMPT, 4) if t < PROMPT_TILES else slice(PROMPT + t - 4, TOK, 2)
            return slice(t * P, (t + 1) * P)

        def block_end(b):
            name = blocks[b][0]
            return plan.unit_no[("unit", name, 7 if name[0] in "gy" else TILES - 1)] + 1

        def queries(u):
            _, t, segs = units[u]
            kv, first = divmod(segs[0][0], A_GROUP)
            rows = slice(kv * HD, (kv + 1) * HD)
            return qT_a[rows, first:first + len(segs), t * P:(t + 1) * P], rows

        mix_order = [s[1] for s in steps if s[0] == "mix_hi"]

        block = ctx.enter_context(nc.Block())

        @block.sync
        def _(sp):
            def load_chunks(ns):
                for n in ns:
                    if n >= RING:
                        sp.wait_ge(unit_done, block_end(plan.owner[n - RING]))
                    at = 0
                    for matrix, row, col, width in plan.chunks[n]:
                        sp.dma_start(ring_whole[:, n % RING, at:at + width],
                                     matrices[matrix][row:row + P, col:col + width]).then_inc(landed[n % RING], 16)
                        at += width

            def load_x(t):
                sp.dma_start(x_in[:, t, :], x_rows(t)).then_inc(x_landed[t], 16)

            load_x(0)
            sp.dma_start(gain_bc[:, :], g_mix[0].partition_broadcast(P)).then_inc(gain_in, 16)
            sp.dma_start(ident[:, :], ident_tab).then_inc(ident_in, 16)
            load_chunks((0, 1))
            load_x(1)
            load_chunks(range(2, KC))
            sp.dma_start(rope_raw[:, :, :, :], rope_a_tab).then_inc(rope_in, 16)
            sp.dma_start(qk_gain[:, 0, :], q_gain[0].partition_broadcast(P)).then_inc(rope_in, 16)
            sp.dma_start(qk_gain[:, 1, :], k_gain[0].partition_broadcast(P)).then_inc(rope_in, 16)
            for t in range(2, TILES):
                load_x(t)
            load_chunks(range(KC, 2 * KC))
            sp.dma_start(band_mask[:, :], mask_tab[:, 0:3 * P]).then_inc(tables_in, 16)
            sp.dma_start(class_mask[:, :, :],
                         mask_tab[:, 3 * P:].rearrange("p (m c) -> p m c", m=3)).then_inc(tables_in, 16)
            sp.dma_start(rope_b[:, :, :, :], rope_b_tab).then_inc(tables_in, 16)
            load_chunks(range(2 * KC, N_CHUNKS))

            sp.wait_ge(unit_done, block_end(plan.index["wo0"]))
            with sp.Fori(0, MLP_STEPS) as i:
                for c in range(2 * KC):
                    if c == 0:
                        sp.wait_ge(scored, i * 8 + len(units))
                    if c == KC:
                        sp.wait_ge(unit_done, i * (2 * TILES) + N_UNITS)
                    src = w_up[c * P:(c + 1) * P, bass.ds(i * COLS, COLS)] if c < KC else \
                        w_down[bass.ds(i * COLS + (c % 4) * P, P), (c - KC) // 4 * COLS:((c - KC) // 4 + 1) * COLS]
                    slot = (N_CHUNKS + c) % RING
                    sp.dma_start(ring_whole[:, slot, :], src).then_inc(landed[slot], 16)
            for t in range(TILES):
                sp.wait_ge(y_ready, t + 1)
                sp.dma_start(y_rows(t), x2[:, t, :]).then_inc(y_out, 16)
            sp.wait_ge(y_out, 16 * TILES)

        @block.gpsimd
        def _(pool):
            def cut_lo(slot):
                pool.tensor_tensor(ring_lo[:, slot, :], ring_whole[:, slot, :], ring_hi[:, slot, :].bitcast(F32),
                                   ALU.subtract).then_inc(lo_cut, 1)

            for s in steps:
                if s[0] == "hi":
                    n = s[1]
                    pool.wait_ge(hi_cut, n + 1)
                    cut_lo(n % RING)
                elif s[0] == "mix_lo" and s[1] < 4:
                    c = s[1]
                    pool.wait_ge(mix_hi, mix_order.index(c) + 1)
                    pool.tensor_tensor(act_lo[:, c, :], mixed_0[:, c, :], act_hi[:, c, :].bitcast(F32),
                                       ALU.subtract).then_inc(mix_ready_0, 1)
            with pool.Fori(0, MLP_STEPS) as i:
                for c in range(2 * KC):
                    n = N_CHUNKS + c
                    pool.wait_ge(hi_cut, i * (2 * KC) + n + 1)
                    cut_lo(n % RING)

        @block.tensor
        def _(pe):
            def split_product(out, sta, mov, first, last):
                pe.matmul(out, sta[0], mov[0], start=first, stop=False)
                pe.matmul(out, sta[0], mov[1], start=False, stop=False)
                return pe.matmul(out, sta[1], mov[0], start=False, stop=last)

            def ring(slot, cols=slice(0, COLS)):
                return ring_hi[:, slot, cols], ring_lo[:, slot, cols]

            begun = {}

            def unit(name, i, end):
                n = plan.unit_no[("unit", name, i)]
                begin = begun.get(n, 0)
                begun[n] = end
                if begin == 0:
                    wait_bank(pe, unit_free, n)
                out = unit_ps[n % 2]
                first_chunk, size = plan.start[name], plan.size[name]
                token_major = name[:2] not in ("ga", "gb", "ya", "yb")
                if name == "qa" and begin == 0:
                    pe.wait_ge(*free_of(turn_free, plan.turn_no[("turn", i, 1)]))
                if name == "ya0" and i == 0:
                    for t in (TILES - 2, TILES - 1):
                        pe.wait_ge(*free_of(turn_free, plan.turn_no[("turn_a", t)]))
                if name == "yb0" and i == 0:
                    for c in range(2):
                        pe.wait_ge(*free_of(turn_free, plan.turn_no[("turn_b", 1, c)]))
                for k in range(begin, end):
                    if i == 0:
                        pe.wait_ge(lo_cut, first_chunk + k + 1)
                    if name == "wo0" and i == 0:
                        pe.wait_ge(*((mix_ready_0, k + 1) if k < 4 else (mix_ready_1, k - 3)))
                    slot = (first_chunk + k) % RING
                    if token_major:
                        cols = tokens_of(name, i)
                        last = split_product(out[:, :], (act_hi[:, k, cols], act_lo[:, k, cols]), ring(slot),
                                             k == 0, k == size - 1)
                    else:
                        c, h = i // 2, i % 2
                        hi, lo = {"g": (act_hi, act_lo), "a": (oTa_hi, oTa_lo),
                                  "b": (oTb_hi, oTb_lo)}[name[0] if name[0] == "g" else name[1]]
                        cols = slice(h * HALF, (h + 1) * HALF)
                        last = split_product(out[:, 0:HALF], ring(slot, slice(c * P, (c + 1) * P)),
                                             (hi[:, k, cols], lo[:, k, cols]), k == 0, k == size - 1)
                return last

            even_count = [0]
            taken = set()

            def scores(u, first):
                branch, t, segs = units[u]
                bank = score_ps[u % 2]
                even = [j for j, seg in enumerate(segs) if branch == "A" or seg[0] % 2 == 0]
                odd = [j for j in range(len(segs)) if j not in even]
                heads = even + odd
                if first:
                    taken.add(u)
                    heads = even or odd
                    pe.wait_ge(maxed, u - 1)
                elif u in taken:
                    heads = odd if even else []
                if branch == "A":
                    pe.wait_ge(queries_split, u + 1)
                if first or u not in taken:
                    names = {"A": ["qa", "kva"], "0": ["qk0"], "1": ["qk1"], "2": ["qk2"]}[branch]
                    for name in names:
                        for tt in {t} | {seg[1] + seg[2] - 1 for seg in segs}:
                            pe.wait_ge(*free_of(turn_free, plan.turn_no[("turn_qk", name, tt)]))
                for j in heads:
                    h, k0, nk = segs[j]
                    at = j * nk * P
                    if even and odd and j == odd[0]:
                        even_count[0] += 1
                        pe.wait_ge(even_heads, even_count[0])
                    out = bank[:, at:at + nk * P]
                    if branch == "A":
                        k = kT_a[:, h // A_GROUP, k0 * P:(k0 + nk) * P]
                        pe.matmul(out, q_hi[:, u % 2, j, :], k, start=True, stop=False)
                        last = pe.matmul(out, q_lo[:, u % 2, j, :], k, start=False, stop=True)
                    else:
                        rows = slice(h % 2 * HD, (h % 2 + 1) * HD)
                        if branch == "0":
                            q = qkT_0[rows, h // 2, t * P:(t + 1) * P]
                            k = qkT_0[rows, 2 + h // 2, k0 * P:(k0 + nk) * P]
                        else:
                            q = qkT_c[rows, t % 2, h // 2 * P:(h // 2 + 1) * P]
                            k = qkT_c[rows, t % 2, (2 + h // 2) * P:(3 + h // 2) * P]
                        last = pe.matmul(out, q, k, start=True, stop=True)
                    if even and odd and j == even[-1]:
                        last.then_inc(even_heads, 1)
                    if j == (even + odd)[-1]:
                        last.then_inc(scored, 1)

            def turn_p(u):
                n = plan.turn_no[("turn_p", u)]
                width = sum(seg[2] for seg in units[u][2])
                pe.wait_ge(expd, u + 1)
                wait_bank(pe, turn_free, n)
                for b in range(width):
                    last = pe.transpose(turn_ps[n % 2][:, b * P:(b + 1) * P],
                                        probs[:, u % 2, b * P:(b + 1) * P], ident[:, :])
                last.then_inc(turned, 1)

            def pv(u):
                branch, t, segs = units[u]
                pe.wait_ge(*free_of(turn_free, plan.turn_no[("turn_p", u)]))
                if u >= 2:
                    pe.wait_ge(out_read, u - 1)
                b = 0
                for s, (h, k0, nk) in enumerate(segs):
                    for j in range(nk):
                        if branch == "A":
                            v = v_a[:, k0 + j, :]
                        else:
                            first = int(branch) * GW + h // 2 * P
                            v = v_b[:, k0 + j, first:first + P]
                        last = pe.matmul(out_ps[u % 2][:, s * P:(s + 1) * P], probsT[:, u % 2, b * P:(b + 1) * P],
                                         v, start=(j == 0), stop=(j == nk - 1))
                        b += 1
                last.then_inc(out_done, 1)

            def up(i, v):
                h, c = v // 4, v % 4
                if v >= 2:
                    pe.wait_ge(u_squared[v % 2], i * 4 + v // 2)
                for k in range(KC):
                    if v == 0:
                        pe.wait_ge(lo_cut, i * (2 * KC) + N_CHUNKS + k + 1)
                    slot = (FIRST_SLOT + k) % RING
                    cols = slice(h * HALF, (h + 1) * HALF)
                    last = split_product(score_ps[v % 2][:, 0:HALF], ring(slot, slice(c * P, (c + 1) * P)),
                                         (act_hi[:, k, cols], act_lo[:, k, cols]), k == 0, k == KC - 1)
                last.then_inc(scored, 1)

            def down(i, w):
                t, j = w // 2, w % 2
                pe.wait_ge(unit_free[w % 2], i * TILES + (N_UNITS + w) // 2)
                pe.wait_ge(u_ready, i * 8 + 4 * (t // 3 + 1))
                for k in range(4):
                    if t == 0:
                        pe.wait_ge(lo_cut, i * (2 * KC) + N_CHUNKS + KC + 4 * j + k + 1)
                    slot = (FIRST_SLOT + KC + 4 * j + k) % RING
                    cols = slice(t * P, (t + 1) * P)
                    last = split_product(unit_ps[w % 2][:, :], (u_hi[:, k, cols], u_lo[:, k, cols]), ring(slot),
                                         k == 0, k == 3)
                last.then_inc(unit_done, 1)

            for s in steps:
                kind = s[0]
                if kind == "unit":
                    unit(s[1], s[2], plan.size[s[1]]).then_inc(unit_done, 1)
                elif kind == "part":
                    unit(s[1], s[2], s[4])
                elif kind in ("turn", "turn2"):
                    n, t, half = plan.turn_no[s], s[1], s[2]
                    if n == 0:
                        pe.wait_ge(ident_in, 16)
                    pe.wait_ge(xn_ready, t + 1 + (TILES if kind == "turn2" else 0))
                    wait_bank(pe, turn_free, n)
                    src = xn if kind == "turn" else xn2
                    for c in range(4):
                        last = pe.transpose(turn_ps[n % 2][:, c * P:(c + 1) * P],
                                            src[:, t % 2, (4 * half + c) * P:(4 * half + c + 1) * P], ident[:, :])
                    last.then_inc(turned, 1)
                elif kind == "turn_qk":
                    n = plan.turn_no[s]
                    pe.wait_ge(tok_ready, plan.qk_no[s] + 1)
                    wait_bank(pe, turn_free, n)
                    for c in range(1 if s[1] == "kva" else 4):
                        last = pe.transpose(turn_ps[n % 2][:, c * P:(c + 1) * P],
                                            tok[:, plan.qk_no[s] % 2, c * P:(c + 1) * P], ident[:, :])
                    last.then_inc(turned, 1)
                elif kind in ("scores_first", "scores"):
                    scores(s[1], kind == "scores_first")
                elif kind == "turn_p":
                    turn_p(s[1])
                elif kind == "pv":
                    pv(s[1])
                elif kind == "turn_a":
                    n, t = plan.turn_no[s], s[1]
                    pe.wait_ge(out_read, len(units))
                    wait_bank(pe, turn_free, n)
                    for c in range(4):
                        last = pe.transpose(turn_ps[n % 2][:, c * P:(c + 1) * P],
                                            o_a[:, t, c * P:(c + 1) * P], ident[:, :])
                    last.then_inc(turned, 1)
                elif kind == "turn_b":
                    n, seq, c = plan.turn_no[s], s[1], s[2]
                    pe.wait_ge(weighted, B_GROUPS)
                    wait_bank(pe, turn_free, n)
                    tiles = range(PROMPT_TILES) if seq == 0 else range(PROMPT_TILES, TILES)
                    stride, bank = len(tiles), turn_ps[n % 2]
                    for g in range(B_GROUPS):
                        for j, t in enumerate(tiles):
                            cols = slice(j * P, (j + 1) * P) if g == 0 else slice(j, stride * P, stride)
                            last = pe.matmul(bank[:, cols], o_b[:, g, t, c * P:(c + 1) * P], ident[:, :],
                                             start=(g == 0 and j == 0), stop=(g == B_GROUPS - 1 and j == stride - 1),
                                             skip_group_check=True)
                    last.then_inc(turned, 1)

                elif kind == "up":
                    if s[1] % 4 == 0:
                        for half in range(2):
                            pe.wait_ge(*free_of(turn_free, plan.turn_no[("turn2", 2 + 3 * (s[1] // 4), half)]))
                    up(0, s[1])

            for w in range(2 * TILES):
                down(0, w)
            with pe.Fori(1, MLP_STEPS) as i:
                for v in range(8):
                    up(i, v)
                for w in range(2 * TILES):
                    down(i, w)

        @block.scalar
        def _(act):
            act.wait_ge(dve_step, 1)
            class_at = [u for u, (branch, _, _) in enumerate(units) if branch in "12"]
            class_units = [units[u][:2] for u in class_at]
            band_end = max(u for u, unit in enumerate(units) if unit[0] == "0") + 1

            act.activation(rms[:, 0:1], eps[:, :], ACT.Sqrt)

            def cut_hi(slot):
                act.activation(ring_hi[:, slot, :], ring_whole[:, slot, :], ACT.Copy).then_inc(hi_cut, 1)

            def cut_mlp(i, c):
                slot = (N_CHUNKS + c) % RING
                act.wait_ge(landed[slot], i * 16 + (plan.landed_total[slot] + 16))
                cut_hi(slot)

            def relu_of(i, v):
                act.wait_ge(scored, i * 8 + (len(units) + v + 1))
                act.activation(relu[:, v % 2, :], score_ps[v % 2][:, 0:HALF], ACT.Relu).then_inc(relu_done, 1)

            def norm(x_ap, junk, n):
                act.activation(junk, x_ap, ACT.Square, accum_out=ssq[:, n % 2:n % 2 + 1]).then_inc(squares, 1)
                act.wait_ge(squares, n + 1)
                act.activation(rms[:, n % 2:n % 2 + 1], ssq[:, n % 2:n % 2 + 1], ACT.Sqrt, scale=1.0 / D,
                               bias=eps[:, :]).then_inc(roots, 1)

            def take_unit(name, i):
                n = plan.unit_no[("unit", name, i)]
                bank = unit_ps[n % 2]
                if name in ("qa", "kva", "qk0", "qk1", "qk2"):
                    q = plan.qk_no[("turn_qk", name, i)]
                    act.wait_ge(unit_done, n + 1)
                    if q >= 2:
                        before = next(x for x, m in plan.qk_no.items() if m == q - 2)
                        act.wait_ge(turned, plan.turn_no[before] + 1)
                    if name in ("qa", "kva"):
                        if q:
                            act.wait_ge(qk_squares, q)
                        width = COLS if name == "qa" else A_KV * HD
                        act.activation(qk_sq[:, 0:width], bank[:, 0:width], ACT.Square)
                    if name == "qa":
                        act.activation(tok[:, q % 2, :].rearrange("p (g k d) -> p g k d", g=A_GROUP, k=A_KV),
                                       bank[:, :].rearrange("p (k g d) -> p g k d", k=A_KV, g=A_GROUP),
                                       ACT.Copy).then_inc(unit_free[n % 2], 1)
                    elif name == "kva":
                        act.activation(v_a[:, i, :], bank[:, P:2 * P], ACT.Copy)
                        act.activation(v_b[:, i, 0:GW], bank[:, 2 * P:], ACT.Copy)
                        act.activation(tok[:, q % 2, 0:P], bank[:, 0:P], ACT.Copy).then_inc(unit_free[n % 2], 1)
                    else:
                        act.activation(tok[:, q % 2, :], bank[:, :], ACT.Copy).then_inc(unit_free[n % 2], 1)
                    if name == "kva":
                        if i == 0:
                            act.wait_ge(qk_squares, TILES)
                            act.activation(q_scale[:, :], q_scale[:, :], ACT.Sqrt,
                                           bias=eps_q[:, :]).then_inc(q_roots, 1)
                        act.wait_ge(qk_squares, q + 1)
                        act.activation(k_rms[:, :], k_ssq[:, :], ACT.Sqrt, scale=1.0 / HD,
                                       bias=eps[:, :]).then_inc(k_roots, 1)
                elif name == "v12":
                    act.wait_ge(unit_done, n + 1)
                    act.activation(v_b[:, i, GW:], bank[:, :], ACT.Copy).then_inc(unit_free[n % 2], 1)
                elif name[0] == "g":
                    order = ["ga0", "gb0", "gb1", "ga1"].index(name)
                    if order == 0:
                        act.wait_ge(scored, band_end)
                    else:
                        act.wait_ge(*free_of(unit_free, plan.unit_no[("unit", ["ya0", "yb0", "yb1"][order - 1], i)]))
                    act.wait_ge(unit_done, n + 1)
                    act.activation(gate[:, i // 2, i % 2 * HALF:(i % 2 + 1) * HALF], bank[:, 0:HALF], ACT.Tanh,
                                   scale=0.5).then_inc(unit_free[n % 2], 1)

            for s in steps:
                kind = s[0]
                if kind == "hi":
                    n = s[1]
                    act.wait_ge(landed[n % RING], plan.landed[n])
                    cut_hi(n % RING)
                elif kind == "norm":
                    t = s[1]
                    act.wait_ge(x_landed[t], 16)
                    if t >= 2:
                        act.wait_ge(turned, plan.turn_no[("turn", t - 2, 1)] + 1)
                    norm(x_in[:, t, :], xn[:, t % 2, :], t)
                elif kind == "norm2":
                    t = s[1]
                    act.wait_ge(*free_of(unit_free, plan.unit_no[("unit", "wo1", t)]))
                    if t >= 2:
                        act.wait_ge(turned, plan.turn_no[("turn2", t - 2, 1)] + 1)
                    norm(x2[:, t, :], xn2[:, t % 2, :], TILES + t)
                elif kind in ("turn", "turn2"):
                    n, t, half = plan.turn_no[s], s[1], s[2]
                    act.wait_ge(turned, n + 1)
                    act.activation(act_hi[:, 4 * half:4 * half + 4, t * P:(t + 1) * P],
                                   turn_ps[n % 2][:, :].rearrange("p (c t) -> p c t", c=4),
                                   ACT.Copy).then_inc(turn_hi, 1)
                elif kind == "turn_qk":
                    n, name, t = plan.turn_no[s], s[1], s[2]
                    act.wait_ge(turned, n + 1)
                    if name in ("qk1", "qk2"):
                        order = class_units.index((name[2], t))
                        if order >= 2:
                            act.wait_ge(scored, class_at[order - 2] + 1)
                        dst = qkT_c[:, t % 2, :]
                    elif name == "qa":
                        dst = qT_a[:, :, t * P:(t + 1) * P]
                    elif name == "kva":
                        for kv in range(A_KV):
                            rows = slice(kv * HD, (kv + 1) * HD)
                            last = act.activation(kT_a[rows, kv, t * P:(t + 1) * P], turn_ps[n % 2][rows, 0:P],
                                                  ACT.Copy)
                        last.then_inc(keys_hi, 1)
                        continue
                    else:
                        dst = qkT_0[:, :, t * P:(t + 1) * P]
                    src = turn_ps[n % 2][:, :]
                    if name in ("qa", "qk0"):
                        src = src.rearrange("p (c t) -> p c t", c=4)
                    act.activation(dst, src, ACT.Copy).then_inc(turn_free[n % 2], 1)
                elif kind == "unit":
                    take_unit(s[1], s[2])
                elif kind == "q_split":
                    u = s[1]
                    _, t, segs = units[u]
                    act.wait_ge(*free_of(turn_free, plan.turn_no[("turn_qk", "qa", t)]))
                    if u >= 2:
                        act.wait_ge(scored, u - 1)
                    for out in range(2):
                        last = act.activation(q_hi[out * HD:(out + 1) * HD, u % 2, 0:len(segs), :], queries(u)[0],
                                              ACT.Copy)
                    last.then_inc(queries_hi, 1)
                elif kind == "scores":
                    u = s[1]
                    branch, t, segs = units[u]
                    act.wait_ge(maxed, u + 1)
                    if branch == "A" and u >= 2:
                        act.wait_ge(turned, plan.turn_no[("turn_p", u - 2)] + 1)
                    src = score_ps[u % 2] if branch == "A" else probs[:, u % 2, :]
                    at = 0
                    for j, (h, k0, nk) in enumerate(segs):
                        col = stat_col(branch, t, h)
                        last = act.activation(probs[:, u % 2, at:at + nk * P], src[:, at:at + nk * P], ACT.Exp,
                                              bias=neg_max[:, col:col + 1],
                                              scale=q_scale[:, col:col + 1] if branch == "A" else 1.0,
                                              accum_out=den[:, col:col + 1])
                        at += nk * P
                    last.then_inc(expd, 1)
                elif kind == "turn_p":
                    u, n = s[1], plan.turn_no[s]
                    width = P * sum(seg[2] for seg in units[u][2])
                    act.wait_ge(turned, n + 1)
                    if u >= 2:
                        act.wait_ge(out_done, u - 1)
                    act.activation(probsT[:, u % 2, 0:width], turn_ps[n % 2][:, 0:width],
                                   ACT.Copy).then_inc(turn_free[n % 2], 1)
                elif kind == "turn_a":
                    n, t = plan.turn_no[s], s[1]
                    act.wait_ge(turned, n + 1)
                    act.activation(oTa_hi[:, :, t * P:(t + 1) * P],
                                   turn_ps[n % 2][:, :].rearrange("p (c t) -> p c t", c=4),
                                   ACT.Copy, scale=0.5).then_inc(turn_hi, 1)
                elif kind == "turn_b":
                    n, seq, c = plan.turn_no[s], s[1], s[2]
                    first, width = (0, PROMPT) if seq == 0 else (PROMPT, SAMPLE)
                    act.wait_ge(turned, n + 1)
                    act.activation(oTb_hi[:, c, first:first + width], turn_ps[n % 2][:, 0:width],
                                   ACT.Copy, scale=0.5).then_inc(turn_hi, 1)
                elif kind == "send_stats":
                    act.wait_ge(stats_packed, 4)
                    act.dma_start(stats_dram[0:PROMPT, :].rearrange("(a r) c -> a r c", r=4),
                                  stats_c[:, 0:4, :]).then_inc(stats_out, 16)
                    act.dma_start(stats_dram[PROMPT:, :].rearrange("(a r) c -> a r c", r=2),
                                  stats_c[:, 4:6, :]).then_inc(stats_out, 16)
                elif kind == "fetch_stats":
                    act.wait_ge(stats_out, 32)
                    act.dma_start(stats_n, stats_dram.rearrange("(t p) c -> p t c", p=P)).then_inc(stats_back, 16)
                elif kind == "combine":
                    act.wait_ge(diffs, 3)
                    act.activation(e_g, e_g, ACT.Exp).then_inc(exps_g, 1)
                    act.wait_ge(shares, 3)
                    act.dma_start(weights_dram.rearrange("(t p) c -> p t c", p=P), w_n).then_inc(shares_out, 16)
                elif kind == "fetch_shares":
                    act.wait_ge(shares_out, 16)
                    act.dma_start(w_c[:, 0:4, :],
                                  weights_dram[0:PROMPT, :].rearrange("(a r) c -> a r c", r=4)).then_inc(shares_back, 16)
                    act.dma_start(w_c[:, 4:6, :],
                                  weights_dram[PROMPT:, :].rearrange("(a r) c -> a r c", r=2)).then_inc(shares_back, 16)
                elif kind == "mix_hi":
                    c = s[1]
                    act.wait_ge(mixed_done, 2 * c + 2 if c >= 4 else 8)
                    act.wait_ge(unit_done, block_end(plan.index["ga1"]))
                    act.activation(act_hi[:, c, :], mixed[c // 4][:, c % 4, :], ACT.Copy).then_inc(mix_hi, 1)
                elif kind == "up":
                    v = s[1]
                    relu_of(0, v)
                    for c in ([v - 1] if v else []) + ([v] if v == 7 else []):
                        cut_mlp(0, KC + c)
                    if v == 7:
                        for c in range(KC):
                            cut_mlp(1, c)
                elif kind == "hi_up":
                    cut_mlp(0, s[1])
                elif kind == "load_x":
                    act.wait_ge(mixed_done, 16)
                    for t in range(TILES):
                        act.dma_start(x2[:, t, :], x_rows(t)).then_inc(x2_landed[t], 16)
                    act.dma_start(gain_mlp[:, :], g_mlp[0].partition_broadcast(P)).then_inc(mlp_gains_in, 16)
                    act.dma_start(gain_fin[:, :], g_final.partition_broadcast(P)).then_inc(mlp_gains_in, 16)

            with act.Fori(1, MLP_STEPS - 1) as i:
                for v in range(8):
                    relu_of(i, v)
                    cut_mlp(i, KC + v)
                for c in range(KC):
                    cut_mlp(i + 1, c)
            for v in range(8):
                relu_of(MLP_STEPS - 1, v)
                cut_mlp(MLP_STEPS - 1, KC + v)

            for t in range(TILES):
                n = 2 * TILES + t
                act.wait_ge(*free_of(unit_free, N_UNITS + 2 * TILES * (MLP_STEPS - 1) + 2 * t + 1))
                if t >= 2:
                    act.wait_ge(y_ready, t - 1)
                norm(x2[:, t, :], xn2[:, t % 2, :], n)

        @block.vector
        def _(dve):
            chain = [0]

            def link(ins):
                chain[0] += 1
                ins.then_inc(dve_step, 1)
                dve.wait_ge(dve_step, chain[0])

            dve.memset(eps_q[:, :], HD * EPS)
            link(dve.memset(eps[:, :], EPS))
            assert SCALE * SCALE * HD == 1

            def normed(n, dst, src, gain):
                dve.wait_ge(roots, n + 1)
                link(dve.reciprocal(rms[:, n % 2:n % 2 + 1], rms[:, n % 2:n % 2 + 1]))
                return dve.scalar_tensor_tensor(dst, src, rms[:, n % 2:n % 2 + 1], gain, ALU.mult, ALU.mult)

            def lo_of_turn(hi, lo, src):
                return dve.tensor_tensor(lo, src, hi.bitcast(F32), ALU.subtract)

            def lo_of_half(hi, lo, src):
                return dve.scalar_tensor_tensor(lo, src, 0.5, hi.bitcast(F32), ALU.mult, ALU.subtract)

            def rotate_a(name, t):
                q = plan.qk_no[("turn_qk", name, t)]
                n = plan.unit_no[("unit", name, t)]
                nh = A_HEADS if name == "qa" else A_KV
                width = nh * HD
                buf = tok[:, q % 2, 0:width]
                pos = t % PROMPT_TILES
                cos, sin = (rope_qc, rope_qs) if name == "qa" else (rope_kc, rope_ks)
                dve.wait_ge(*free_of(unit_free, n))
                if q:
                    dve.wait_ge(tok_ready, q)
                sums = q_scale[:, t * A_HEADS:(t + 1) * A_HEADS] if name == "qa" else k_ssq[:, :]
                dve.tensor_reduce(sums, qk_sq[:, 0:width].rearrange("p (h d) -> p h d", d=HD), AX_X,
                                  ALU.add).then_inc(qk_squares, 1)
                heads = buf.rearrange("p (h d) -> p h d", d=HD)
                if name == "kva":
                    if t == 0:
                        dve.wait_ge(q_roots, 1)
                        link(dve.reciprocal(q_scale[:, :], q_scale[:, :]))
                    dve.wait_ge(k_roots, t + 1)
                    link(dve.reciprocal(k_rms[:, :], k_rms[:, :]))
                    link(dve.tensor_tensor(heads, heads, k_rms[:, :].unsqueeze(2).broadcast_to([P, nh, HD]),
                                           ALU.mult))
                pairs = buf.rearrange("p (h a x e) -> p h a x e", h=nh, a=2, x=2)
                turned_pairs = rot[:, 0:width].rearrange("p (h a x e) -> p h a x e", h=nh, a=2, x=2)
                sines = sin[:, pos, :].rearrange("p (a x e) -> p a x e", a=2, x=2)
                for x in range(2):
                    last = dve.tensor_tensor(turned_pairs[:, :, :, x, :], pairs[:, :, :, 1 - x, :],
                                             sines[:, :, x, :].unsqueeze(1).broadcast_to([P, nh, 2, 16]), ALU.mult)
                link(last)
                link(dve.tensor_tensor(heads, heads, cos[:, pos, :].unsqueeze(1).broadcast_to([P, nh, HD]), ALU.mult))
                dve.tensor_tensor(buf, buf, rot[:, 0:width], ALU.add).then_inc(tok_ready, 1)

            def rotate_b(name, t):
                q = plan.qk_no[("turn_qk", name, t)]
                n = plan.unit_no[("unit", name, t)]
                row = t % PROMPT_TILES if name == "qk0" else 4 + t
                front = tok[:, q % 2, :].rearrange("p (h d) -> p h d", d=HD)[:, :, 0:16]
                other = rot[:, 0:P].rearrange("p (h d) -> p h d", d=16)
                cos = rope_b[:, row, 0, :].unsqueeze(1).broadcast_to([P, 8, 16])
                dve.wait_ge(*free_of(unit_free, n))
                dve.wait_ge(tok_ready, q)
                for x in range(2):
                    last = dve.tensor_tensor(other[:, :, 8 * x:8 * x + 8], front[:, :, 8 - 8 * x:16 - 8 * x],
                                             rope_b[:, row, 1, 8 * x:8 * x + 8].unsqueeze(1)
                                             .broadcast_to([P, 8, 8]), ALU.mult)
                link(last)
                link(dve.tensor_tensor(front, front, cos, ALU.mult))
                dve.tensor_tensor(front, front, other, ALU.add).then_inc(tok_ready, 1)

            def square_up(i, v):
                h, c = v // 4, v % 4
                cols = slice(h * HALF, (h + 1) * HALF)
                dve.wait_ge(relu_done, i * 8 + v + 1)
                dve.scalar_tensor_tensor(usq[:, v % 2, :], score_ps[v % 2][:, 0:HALF], 0.0, relu[:, v % 2, :],
                                         ALU.max, ALU.mult).then_inc(u_squared[v % 2], 1)
                dve.wait_ge(u_squared[v % 2], i * 4 + v // 2 + 1)
                dve.tensor_copy(u_hi[:, c, cols], usq[:, v % 2, :]).then_inc(u_cut, 1)
                dve.wait_ge(u_cut, i * 8 + v + 1)
                dve.tensor_tensor(u_lo[:, c, cols], usq[:, v % 2, :], u_hi[:, c, cols].bitcast(F32),
                                  ALU.subtract).then_inc(u_ready, 1)

            def add_down(i, w):
                t, j = w // 2, w % 2
                dve.wait_ge(unit_done, i * (2 * TILES) + (N_UNITS + w + 1))
                part = x2[:, t, j * COLS:(j + 1) * COLS]
                dve.tensor_tensor(part, part, unit_ps[w % 2][:, :], ALU.add).then_inc(unit_free[w % 2], 1)

            def maxima(u):
                branch, t, segs = units[u]
                dve.wait_ge(scored, u + 1)
                ns, width = len(segs), segs[0][2] * P
                col = stat_col(branch, t, segs[0][0])
                cols = neg_max[:, col:col + ns]
                bank = score_ps[u % 2][:, 0:ns * width]
                if branch == "A":
                    link(dve.tensor_reduce(cols, bank.rearrange("p (s w) -> p s w", s=ns), AX_X, ALU.max))
                    dve.scalar_tensor_tensor(cols, cols, -1.0, q_scale[:, col:col + ns], ALU.mult,
                                             ALU.mult).then_inc(maxed, 1)
                    return
                if u >= 2:
                    dve.wait_ge(turned, plan.turn_no[("turn_p", u - 2)] + 1)
                dst = probs[:, u % 2, 0:ns * width]
                if branch == "0":
                    first = (segs[0][1] - t + 1) * P
                    shape = [P, ns, width]
                    mask = band_mask[:, first:first + width]
                    mask = mask.unsqueeze(1).broadcast_to(shape)
                    view = "p (s w) -> p s w"
                    split = dict(s=ns)
                elif branch == "1" and t < PROMPT_TILES:
                    mask = band_mask[:, P:2 * P].unsqueeze(1).broadcast_to([P, ns, width])
                    view, split = "p (s w) -> p s w", dict(s=ns)
                else:
                    m = {("1", False): 0, ("2", True): 1, ("2", False): 2}[(branch, t < PROMPT_TILES)]
                    mask = class_mask[:, m, :].unsqueeze(1).broadcast_to([P, ns * width // 8, 8])
                    view, split = "p (s w) -> p s w", dict(w=8)
                link(dve.scalar_tensor_tensor(dst.rearrange(view, **split), bank.rearrange(view, **split), SCALE,
                                              mask, ALU.mult, ALU.add))
                link(dve.tensor_reduce(cols, dst.rearrange("p (s w) -> p s w", s=ns), AX_X, ALU.max))
                dve.tensor_scalar(cols, cols, -1.0, None, ALU.mult).then_inc(maxed, 1)

            def take_out(u):
                branch, t, segs = units[u]
                ns, h = len(segs), segs[0][0]
                col = stat_col(branch, t, h)
                src = out_ps[u % 2][:, 0:ns * P].rearrange("p (s w d) -> p s w d", w=2, d=HD)
                dve.wait_ge(out_done, u + 1)
                if branch == "A":
                    link(dve.reciprocal(den[:, col:col + ns], den[:, col:col + ns]))
                    dve.tensor_tensor(o_a[:, t, h * HD:(h + ns) * HD].rearrange("p (s d) -> p s d", d=HD),
                                      src[:, :, h // A_GROUP, :],
                                      den[:, col:col + ns].unsqueeze(2).broadcast_to([P, ns, HD]),
                                      ALU.mult).then_inc(out_read, 1)
                else:
                    dst = o_b[:, int(branch), t, h * HD:(h + ns) * HD].rearrange("p (s d) -> p s d", d=HD)
                    for x in range(min(2, ns)):
                        last = dve.tensor_copy(dst[:, x::2, :], src[:, x::2, (h + x) % 2, :])
                    last.then_inc(out_read, 1)

            for s in steps:
                kind = s[0]
                if kind in ("norm", "norm2"):
                    t = s[1]
                    if kind == "norm":
                        dve.wait_ge(x_landed[t], 16)
                        dve.wait_ge(gain_in, 16)
                        normed(t, xn[:, t % 2, :], x_in[:, t, :], gain_bc[:, :]).then_inc(xn_ready, 1)
                    else:
                        dve.wait_ge(mlp_gains_in, 32)
                        normed(TILES + t, xn2[:, t % 2, :], x2[:, t, :], gain_mlp[:, :]).then_inc(xn_ready, 1)
                elif kind == "tables":
                    dve.wait_ge(rope_in, 48)
                    for c, sn, j in ((rope_qc, rope_qs, 0), (rope_kc, rope_ks, 1)):
                        gain = qk_gain[:, j, :].unsqueeze(1).broadcast_to([P, PROMPT_TILES, HD])
                        dve.tensor_tensor(c[:, :, :], rope_raw[:, 0, :, :], gain, ALU.mult)
                        other = qk_gain[:, j, :].rearrange("p (a x e) -> p a x e", a=2, x=2)
                        out = sn[:, :, :].rearrange("p t (a x e) -> p t a x e", a=2, x=2)
                        raw_s = rope_raw[:, 1, :, :].rearrange("p t (a x e) -> p t a x e", a=2, x=2)
                        for x in range(2):
                            last = dve.tensor_tensor(
                                out[:, :, :, x, :], raw_s[:, :, :, x, :],
                                other[:, :, 1 - x, :].unsqueeze(1).broadcast_to([P, PROMPT_TILES, 2, 16]),
                                ALU.mult)
                    link(last)
                elif kind in ("turn", "turn2"):
                    n, t, half = plan.turn_no[s], s[1], s[2]
                    dve.wait_ge(turn_hi, plan.split_no[s] + 1)
                    at = (slice(None), slice(4 * half, 4 * half + 4), slice(t * P, (t + 1) * P))
                    last = lo_of_turn(act_hi[at], act_lo[at],
                                      turn_ps[n % 2][:, :].rearrange("p (c t) -> p c t", c=4))
                    last.then_inc(turn_free[n % 2], 1)
                elif kind == "unit":
                    name, i = s[1], s[2]
                    n = plan.unit_no[s]
                    if name in ("qa", "kva"):
                        rotate_a(name, i)
                    elif name in ("qk0", "qk1", "qk2"):
                        dve.wait_ge(tables_in, 48)
                        rotate_b(name, i)
                    elif name[0] == "y":
                        c, h = i // 2, i % 2
                        cols = slice(h * HALF, (h + 1) * HALF)
                        into = mixed[int(name[2])][:, c, cols]
                        dve.wait_ge(*free_of(unit_free, plan.unit_no[("unit", "g" + name[1:], i)]))
                        dve.wait_ge(unit_done, n + 1)
                        if name in ("ya0", "yb1"):
                            dve.scalar_tensor_tensor(into, gate[:, c, cols], 1.0, unit_ps[n % 2][:, 0:HALF],
                                                     ALU.add, ALU.mult).then_inc(unit_free[n % 2], 1)
                        else:
                            part = mix_part[:, i % 2, :]
                            dve.scalar_tensor_tensor(part, gate[:, c, cols], 1.0, unit_ps[n % 2][:, 0:HALF],
                                                     ALU.add, ALU.mult).then_inc(unit_free[n % 2], 1)
                            dve.wait_ge(*free_of(unit_free, n))
                            dve.tensor_tensor(into, into, part, ALU.add).then_inc(mixed_done, 1)
                    elif name[:2] == "wo":
                        j = int(name[2])
                        dve.wait_ge(unit_done, n + 1)
                        if j == 0:
                            dve.wait_ge(x2_landed[i], 16)
                        part = x2[:, i, j * COLS:(j + 1) * COLS]
                        dve.tensor_tensor(part, part, unit_ps[n % 2][:, :], ALU.add).then_inc(unit_free[n % 2], 1)
                elif kind == "turn_qk" and s[1] == "kva":
                    n, t = plan.turn_no[s], s[2]
                    dve.wait_ge(keys_hi, t + 1)
                    for kv in range(A_KV):
                        rows, other = slice(kv * HD, (kv + 1) * HD), slice((1 - kv) * HD, (2 - kv) * HD)
                        last = dve.tensor_tensor(kT_a[other, kv, t * P:(t + 1) * P], turn_ps[n % 2][rows, 0:P],
                                                 kT_a[rows, kv, t * P:(t + 1) * P].bitcast(F32), ALU.subtract)
                    last.then_inc(turn_free[n % 2], 1)
                elif kind == "q_split":
                    u = s[1]
                    heads, (source, rows) = len(units[u][2]), queries(u)
                    dve.wait_ge(queries_hi, u + 1)
                    for out in range(2):
                        last = dve.tensor_tensor(q_lo[out * HD:(out + 1) * HD, u % 2, 0:heads, :], source,
                                                 q_hi[rows, u % 2, 0:heads, :].bitcast(F32), ALU.subtract)
                    last.then_inc(queries_split, 1)
                elif kind == "scores":
                    maxima(s[1])
                elif kind == "pv":
                    take_out(s[1])
                elif kind == "send_stats":
                    dve.wait_ge(expd, len(units))
                    for j, (src, g) in enumerate(((neg_max, 1), (neg_max, 2), (den, 1), (den, 2))):
                        first = STAT_A + g * STAT_B
                        dve.tensor_copy(stats_c[:, :, 4 * j:4 * j + 4],
                                        src[:, first:first + STAT_B].rearrange("p (t h) -> p t h", h=4))\
                           .then_inc(stats_packed, 1)
                elif kind == "turn_a":
                    n, t = plan.turn_no[s], s[1]
                    dve.wait_ge(turn_hi, plan.split_no[s] + 1)
                    at = (slice(None), slice(0, 4), slice(t * P, (t + 1) * P))
                    lo_of_half(oTa_hi[at], oTa_lo[at], turn_ps[n % 2][:, :].rearrange("p (c t) -> p c t", c=4))\
                        .then_inc(turn_free[n % 2], 1)
                elif kind == "turn_b":
                    n, seq, c = plan.turn_no[s], s[1], s[2]
                    first, width = (0, PROMPT) if seq == 0 else (PROMPT, SAMPLE)
                    dve.wait_ge(turn_hi, plan.split_no[s] + 1)
                    at = (slice(None), c, slice(first, first + width))
                    lo_of_half(oTb_hi[at], oTb_lo[at], turn_ps[n % 2][:, 0:width]).then_inc(turn_free[n % 2], 1)
                elif kind == "combine":
                    dve.wait_ge(stats_back, 16)
                    own = slice(STAT_A, STAT_A + STAT_B)
                    m = [neg_max[:, own].rearrange("p (t h) -> p t h", h=4), stats_n[:, :, 0:4], stats_n[:, :, 4:8]]
                    d = [den[:, own].rearrange("p (t h) -> p t h", h=4), stats_n[:, :, 8:12], stats_n[:, :, 12:16]]
                    top, total = small[:, 0], small[:, 1]
                    link(dve.tensor_tensor(top, m[0], m[1], ALU.min))
                    link(dve.tensor_tensor(top, top, m[2], ALU.min))
                    for g in range(B_GROUPS):
                        dve.tensor_tensor(e_g[:, g], top, m[g], ALU.subtract).then_inc(diffs, 1)
                    dve.wait_ge(exps_g, 1)
                    for g in range(B_GROUPS):
                        link(dve.tensor_tensor(z_g[:, g], e_g[:, g], d[g], ALU.mult))
                    link(dve.tensor_tensor(total, z_g[:, 0], z_g[:, 1], ALU.add))
                    link(dve.tensor_tensor(total, total, z_g[:, 2], ALU.add))
                    link(dve.reciprocal(total, total))
                    for g, out in enumerate((w_0, w_n[:, :, 0:4], w_n[:, :, 4:8])):
                        dve.tensor_tensor(out, e_g[:, g], total, ALU.mult).then_inc(shares, 1)
                elif kind == "weight":
                    dve.wait_ge(shares, 1)
                    for g, share in enumerate((w_0, w_c[:, :, 0:4], w_c[:, :, 4:8])):
                        if g == 1:
                            dve.wait_ge(shares_back, 32)
                        part = o_b[:, g].rearrange("p t (h d) -> p t h d", d=HD)
                        dve.tensor_tensor(part, part, share.unsqueeze(3).broadcast_to([P, TILES, B_HEADS, HD]),
                                          ALU.mult).then_inc(weighted, 1)
                elif kind == "up":
                    square_up(0, s[1])
                elif kind == "mix_lo" and s[1] >= 4:
                    c = s[1]
                    dve.wait_ge(mix_hi, mix_order.index(c) + 1)
                    dve.tensor_tensor(act_lo[:, c, :], mixed_1[:, c - 4, :], act_hi[:, c, :].bitcast(F32),
                                      ALU.subtract).then_inc(mix_ready_1, 1)

            def output(t):
                normed(2 * TILES + t, x2[:, t, :], x2[:, t, :], gain_fin[:, :]).then_inc(y_ready, 1)

            for w in range(2 * TILES):
                add_down(0, w)
            with dve.Fori(1, MLP_STEPS - 1) as i:
                for v in range(8):
                    square_up(i, v)
                for w in range(2 * TILES):
                    add_down(i, w)
            for v in range(8):
                square_up(MLP_STEPS - 1, v)
            for w in range(2 * TILES):
                add_down(MLP_STEPS - 1, w)
                if w >= 3 and w % 2:
                    output(w // 2 - 1)
            output(TILES - 1)


def rope_angles(pos, dim, theta):
    freqs = np.float32(theta) ** (-(np.arange(dim // 2, dtype=np.float32) * np.float32(2.0)) / np.float32(dim))
    return pos.astype(np.float32)[:, None] * freqs[None, :].astype(np.float32)


def shape_tables():
    pos = np.arange(PROMPT)
    row, col = rope_angles(pos // 64, HD // 2, 10000.0), rope_angles(pos % 64, HD // 2, 10000.0)
    cos = np.concatenate([np.cos(row), np.cos(row), np.cos(col), np.cos(col)], 1)
    sin = np.concatenate([-np.sin(row), np.sin(row), -np.sin(col), np.sin(col)], 1)
    a = np.stack([cos, sin]).reshape(2, PROMPT_TILES, P, HD).transpose(2, 0, 1, 3)
    rows = np.arange(P)
    order = [t * P + rows for t in range(4)] + [4 * rows + r for r in range(4)] + [2 * rows + r for r in range(2)]
    b = []
    for p in order:
        ang = rope_angles(p, 16, 500000.0)
        b.append(np.stack([np.concatenate([np.cos(ang), np.cos(ang)], 1),
                           np.concatenate([-np.sin(ang), np.sin(ang)], 1)], 1))
    b = np.stack(b, 1)
    keys = np.arange(3 * P) - P
    band = np.where(np.abs(keys[None, :] - rows[:, None]) <= 64, 0.0, NEG)
    same = [np.where(rows[:, None] % m == np.arange(8)[None, :] % m, 0.0, NEG) for m in (2, 4, 8)]
    mask = np.concatenate([band] + same, 1)
    out = {"rope_a_tab": a, "rope_b_tab": b, "mask_tab": mask, "ident_tab": np.eye(P)}
    return {k: np.ascontiguousarray(v, dtype=np.float32) for k, v in out.items()}


_INS = ["x_prompt", "x_sample", "w_in", "w_a_out", "w_b_out", "w_out", "g_mix", "q_gain", "k_gain", "g_mlp",
        "w_up", "w_down", "g_final"]
_TABLES = ["rope_a_tab", "rope_b_tab", "mask_tab", "ident_tab"]


def kernel(**inputs):
    import concourse.bacc as bacc
    from concourse.bass_utils import run_bass_kernel_spmd

    nc = bacc.Bacc("TRN2", target_bir_lowering=False, num_devices=1)
    arrays, args = {}, []
    tables = shape_tables()
    for name in _INS + _TABLES:
        a = np.ascontiguousarray(inputs[name] if name in inputs else tables[name])
        arrays[f"in_{name}"] = a
        args.append(nc.dram_tensor(f"in_{name}", a.shape, mybir.dt.from_np(a.dtype), kind="ExternalInput").ap())
    for name, n in (("y_prompt", PROMPT), ("y_sample", SAMPLE)):
        args.append(nc.dram_tensor(name, (1, n, D), F32, kind="ExternalOutput").ap())
    build(nc, *args)
    r = run_bass_kernel_spmd(nc, [arrays], core_ids=[0])
    return r.results[0]["y_prompt"], r.results[0]["y_sample"]
```
